# Optimizing a Trainium2 kernel written in Bass

```python
import jax, jax.numpy as jnp
from jax import lax
import numpy as np

D_MODEL = 1024
BATCH = 1
SEQ = 512
DEPTH = 1

D_MIX = D_MODEL
EPS = 1e-6
GLA_HEADS = 4
GLA_DK = D_MODEL // 32
GLA_DV = D_MODEL // 16
GLA_QK = GLA_HEADS * GLA_DK
GLA_W = GLA_HEADS * GLA_DV
GLA_RANK = 16
GLA_TAU = 16.0
GLA_CHUNK = 64
FNET_GROUPS = 4
FNET_DG = D_MODEL // 16
FNET_W = FNET_GROUPS * FNET_DG
MLA_HEADS = 8
MLA_NOPE = D_MODEL // 16
MLA_ROPE = D_MODEL // 32
MLA_V = D_MODEL // 16
MLA_Q_RANK = D_MODEL // 4
MLA_KV_RANK = D_MODEL // 8
MLA_W = MLA_HEADS * MLA_V
ROPE_THETA = 10000.0
Q_BLOCK = 128
IN_SPLITS = (GLA_QK, GLA_QK, GLA_W, GLA_W, GLA_RANK, GLA_RANK, FNET_W, MLA_Q_RANK, MLA_KV_RANK, MLA_ROPE)
IN_WIDTH = GLA_QK * 2 + GLA_W * 2 + GLA_RANK * 2 + FNET_W + MLA_Q_RANK + MLA_KV_RANK + MLA_ROPE
N_GROUPS = 4
EXPERTS_PER_GROUP = 8
N_EXPERTS = N_GROUPS * EXPERTS_PER_GROUP
TOP_K = 2
D_EXPERT = D_MODEL // 4

kernel_name = "hybrid_gla_fnet_mla_hmoe_encoder"

def rms_norm(x, g):
    xf = x.astype(jnp.float32)
    y = xf * lax.rsqrt(jnp.mean(xf * xf, axis=-1, keepdims=True) + EPS)
    return (y * g.astype(jnp.float32)).astype(x.dtype)

def rope_tables(positions):
    inv = 1.0 / (ROPE_THETA ** (jnp.arange(0, MLA_ROPE, 2, dtype=jnp.float32) / MLA_ROPE))
    ang = positions.astype(jnp.float32)[..., None] * inv
    return jnp.cos(ang), jnp.sin(ang)

def apply_rope(x, cos, sin):
    x1, x2 = jnp.split(x.astype(jnp.float32), 2, axis=-1)
    return jnp.concatenate([x1 * cos - x2 * sin, x1 * sin + x2 * cos], axis=-1).astype(x.dtype)

def gla_direction(q, k, v, log_a, inclusive):
    B, S, H, dk = q.shape
    dv = v.shape[-1]
    C = GLA_CHUNK
    N = S // C
    f32 = jnp.float32
    qc = q.astype(f32).reshape(B, N, C, H, dk)
    kc = k.astype(f32).reshape(B, N, C, H, dk)
    vc = v.astype(f32).reshape(B, N, C, H, dv)
    b = jnp.cumsum(log_a.reshape(B, N, C, H, dk), axis=2)
    b_last = b[:, :, -1]
    q_dec = qc * jnp.exp(b)
    k_inv = kc * jnp.exp(-b)
    k_end = kc * jnp.exp(b_last[:, :, None] - b)
    mask = jnp.tril(jnp.ones((C, C), dtype=bool), 0 if inclusive else -1)
    att = jnp.where(mask, jnp.einsum('bnihd,bnjhd->bnhij', q_dec, k_inv), 0.0)
    o_intra = jnp.einsum('bnhij,bnjhv->bnihv', att, vc)
    kv = jnp.einsum('bnjhd,bnjhv->nbhdv', k_end, vc)
    decay = jnp.exp(b_last).transpose(1, 0, 2, 3)

    def step(state, inp):
        kv_n, dec_n = inp
        return dec_n[..., None] * state + kv_n, state

    _, s_prev = lax.scan(step, jnp.zeros((B, H, dk, dv), f32), (kv, decay))
    o_inter = jnp.einsum('bnihd,nbhdv->bnihv', q_dec, s_prev)
    return (o_intra + o_inter).reshape(B, S, H, dv)

def gla_mixer(q, k, v, g, a_f, a_b, wa_f, ba_f, wa_b, ba_b, norm_g):
    B, S, _ = q.shape
    qh = q.reshape(B, S, GLA_HEADS, GLA_DK) * (GLA_DK ** -0.5)
    kh = k.reshape(B, S, GLA_HEADS, GLA_DK)
    vh = v.reshape(B, S, GLA_HEADS, GLA_DV)
    log_af = (jax.nn.log_sigmoid((a_f @ wa_f + ba_f).astype(jnp.float32)) / GLA_TAU).reshape(B, S, GLA_HEADS, GLA_DK)
    log_ab = (jax.nn.log_sigmoid((a_b @ wa_b + ba_b).astype(jnp.float32)) / GLA_TAU).reshape(B, S, GLA_HEADS, GLA_DK)
    o_f = gla_direction(qh, kh, vh, log_af, True)
    o_b = jnp.flip(gla_direction(jnp.flip(qh, 1), jnp.flip(kh, 1), jnp.flip(vh, 1), jnp.flip(log_ab, 1), False), 1)
    o = rms_norm(o_f + o_b, norm_g).reshape(B, S, GLA_W)
    return (o * jax.nn.silu(g.astype(jnp.float32))).astype(q.dtype)

def fnet_mixer(u, w_mix):
    B, S, _ = u.shape
    uf = u.astype(jnp.float32).reshape(B, S, FNET_GROUPS, FNET_DG)
    f = jnp.fft.fft2(uf, axes=(1, 3), norm='ortho').real
    y = jnp.einsum('bsgc,gcd->bsgd', f, w_mix.astype(jnp.float32))
    return y.reshape(B, S, FNET_W).astype(u.dtype)

def mla_mixer(c_q, c_kv, k_r, cos, sin, q_norm_g, w_uq, kv_norm_g, w_ukv):
    B, S, _ = c_q.shape
    q = (rms_norm(c_q, q_norm_g) @ w_uq).reshape(B, S, MLA_HEADS, MLA_NOPE + MLA_ROPE)
    q_nope = q[..., :MLA_NOPE]
    q_rope = apply_rope(q[..., MLA_NOPE:], cos[:, :, None], sin[:, :, None])
    kv = (rms_norm(c_kv, kv_norm_g) @ w_ukv).reshape(B, S, MLA_HEADS, MLA_NOPE + MLA_V)
    k_nope = kv[..., :MLA_NOPE]
    v = kv[..., MLA_NOPE:]
    k_rope = apply_rope(k_r, cos, sin)
    scale = (MLA_NOPE + MLA_ROPE) ** -0.5
    nb = S // Q_BLOCK
    qn_blocks = q_nope.reshape(B, nb, Q_BLOCK, MLA_HEADS, MLA_NOPE).transpose(1, 0, 2, 3, 4)
    qr_blocks = q_rope.reshape(B, nb, Q_BLOCK, MLA_HEADS, MLA_ROPE).transpose(1, 0, 2, 3, 4)

    def attend(blk):
        qn, qr = blk
        s = (jnp.einsum('bqhd,bkhd->bhqk', qn, k_nope, preferred_element_type=jnp.float32)
             + jnp.einsum('bqhr,bkr->bhqk', qr, k_rope, preferred_element_type=jnp.float32)) * scale
        p = jax.nn.softmax(s, axis=-1)
        return jnp.einsum('bhqk,bkhv->bqhv', p.astype(v.dtype), v)

    o = lax.map(attend, (qn_blocks, qr_blocks))
    return o.transpose(1, 0, 2, 3, 4).reshape(B, S, MLA_W)

def hier_moe(h, w_rg, b_rg, w_re, b_re, w_gate, w_up, w_down):
    B, S, D = h.shape
    t = h.reshape(B * S, D)
    f32 = jnp.float32
    grp_p = jax.nn.softmax((t @ w_rg + b_rg).astype(f32), axis=-1)
    grp_w, grp_idx = lax.top_k(grp_p, 1)
    exp_logits = (t @ w_re + b_re).astype(f32).reshape(-1, N_GROUPS, EXPERTS_PER_GROUP)
    in_grp = jnp.einsum('tg,tge->te', jax.nn.one_hot(grp_idx[:, 0], N_GROUPS, dtype=f32), exp_logits)
    e_w, e_idx = lax.top_k(jax.nn.softmax(in_grp, axis=-1), TOP_K)
    e_w = e_w / jnp.sum(e_w, axis=-1, keepdims=True)
    expert_id = grp_idx * EXPERTS_PER_GROUP + e_idx
    combine = jnp.sum(jax.nn.one_hot(expert_id, N_EXPERTS, dtype=f32) * (grp_w * e_w)[..., None], axis=1)
    y = jnp.zeros(t.shape, f32)
    for e in range(N_EXPERTS):
        he = jax.nn.silu(t @ w_gate[e]) * (t @ w_up[e])
        y = y + combine[:, e:e + 1] * (he @ w_down[e]).astype(f32)
    return y.reshape(B, S, D).astype(h.dtype)

def setup_inputs(seed: int = 0) -> dict:
    key = jax.random.key(seed)
    ks = jax.random.split(key, 32)
    nrm = lambda k, shape, s: jax.random.normal(k, shape, jnp.float32) * s
    gain = lambda k, shape: 1.0 + 0.02 * jax.random.normal(k, shape, jnp.float32)
    L = DEPTH
    x = jax.random.normal(ks[0], (BATCH, SEQ, D_MODEL), jnp.float32)
    positions = (jnp.arange(SEQ, dtype=jnp.int32)[None, :]
                 + jax.random.randint(ks[1], (BATCH, 1), 0, 1024, dtype=jnp.int32))
    return {
        "x": x,
        "positions": positions,
        "norm1_g": gain(ks[2], (L, D_MODEL)),
        "w_in": nrm(ks[3], (L, D_MODEL, IN_WIDTH), D_MODEL ** -0.5),
        "gla_wa_f": nrm(ks[4], (L, GLA_RANK, GLA_QK), GLA_RANK ** -0.5),
        "gla_ba_f": nrm(ks[5], (L, GLA_QK), 0.1),
        "gla_wa_b": nrm(ks[6], (L, GLA_RANK, GLA_QK), GLA_RANK ** -0.5),
        "gla_ba_b": nrm(ks[7], (L, GLA_QK), 0.1),
        "gla_norm_g": gain(ks[8], (L, GLA_DV)),
        "fnet_w": nrm(ks[9], (L, FNET_GROUPS, FNET_DG, FNET_DG), FNET_DG ** -0.5),
        "mla_q_norm_g": gain(ks[10], (L, MLA_Q_RANK)),
        "mla_w_uq": nrm(ks[11], (L, MLA_Q_RANK, MLA_HEADS * (MLA_NOPE + MLA_ROPE)), MLA_Q_RANK ** -0.5),
        "mla_kv_norm_g": gain(ks[12], (L, MLA_KV_RANK)),
        "mla_w_ukv": nrm(ks[13], (L, MLA_KV_RANK, MLA_HEADS * (MLA_NOPE + MLA_V)), MLA_KV_RANK ** -0.5),
        "w_out": nrm(ks[14], (L, D_MIX, D_MODEL), D_MIX ** -0.5),
        "norm2_g": gain(ks[15], (L, D_MODEL)),
        "moe_w_rg": nrm(ks[16], (L, D_MODEL, N_GROUPS), D_MODEL ** -0.5),
        "moe_b_rg": nrm(ks[17], (L, N_GROUPS), 0.01),
        "moe_w_re": nrm(ks[18], (L, D_MODEL, N_EXPERTS), D_MODEL ** -0.5),
        "moe_b_re": nrm(ks[19], (L, N_EXPERTS), 0.01),
        "moe_w_gate": nrm(ks[20], (L, N_EXPERTS, D_MODEL, D_EXPERT), D_MODEL ** -0.5),
        "moe_w_up": nrm(ks[21], (L, N_EXPERTS, D_MODEL, D_EXPERT), D_MODEL ** -0.5),
        "moe_w_down": nrm(ks[22], (L, N_EXPERTS, D_EXPERT, D_MODEL), D_EXPERT ** -0.5),
        "final_norm_g": gain(ks[23], (D_MODEL,)),
    }

def reference(x, positions, norm1_g, w_in, gla_wa_f, gla_ba_f, gla_wa_b, gla_ba_b, gla_norm_g, fnet_w,
              mla_q_norm_g, mla_w_uq, mla_kv_norm_g, mla_w_ukv, w_out, norm2_g, moe_w_rg, moe_b_rg,
              moe_w_re, moe_b_re, moe_w_gate, moe_w_up, moe_w_down, final_norm_g):
    cos, sin = rope_tables(positions)
    split_at = [int(i) for i in np.cumsum(IN_SPLITS)[:-1]]
    for l in range(DEPTH):
        xn = rms_norm(x, norm1_g[l])
        proj = xn @ w_in[l]
        gq, gk, gv, gg, gaf, gab, fu, cq, ckv, kr = jnp.split(proj, split_at, axis=-1)
        o_gla = gla_mixer(gq, gk, gv, gg, gaf, gab, gla_wa_f[l], gla_ba_f[l], gla_wa_b[l], gla_ba_b[l], gla_norm_g[l])
        o_fnet = fnet_mixer(fu, fnet_w[l])
        o_mla = mla_mixer(cq, ckv, kr, cos, sin, mla_q_norm_g[l], mla_w_uq[l], mla_kv_norm_g[l], mla_w_ukv[l])
        x = x + jnp.concatenate([o_gla, o_fnet, o_mla], axis=-1) @ w_out[l]
        x = x + hier_moe(rms_norm(x, norm2_g[l]), moe_w_rg[l], moe_b_rg[l], moe_w_re[l], moe_b_re[l],
                         moe_w_gate[l], moe_w_up[l], moe_w_down[l])
    return rms_norm(x, final_norm_g)


_drawn_inputs = setup_inputs


def setup_inputs(seed=0):
    import zlib

    import numpy as np

    out = dict(_drawn_inputs(seed))
    spreads = {}
    factors = {'gla_ba_b': 3.368,
     'gla_norm_g': 37.336,
     'mla_q_norm_g': 5.451,
     'mla_kv_norm_g': 8.0,
     'moe_b_rg': 52.168,
     'moe_b_re': 30.048,
     'final_norm_g': 8.45,
     'gla_wa_f': 3.16,
     'gla_ba_f': 6.002,
     'gla_wa_b': 3.155,
     'norm2_g': 8.0}
    for name, (base, spread) in spreads.items():
        noise = np.random.default_rng([zlib.crc32(name.encode()), seed]).standard_normal(out[name].shape)
        drawn = base * np.exp(spread * noise) if base else spread * noise
        out[name] = __import__('jax').numpy.asarray(drawn.astype(out[name].dtype))
    for name, factor in factors.items():
        out[name] = (out[name] * factor).astype(out[name].dtype)
    return out
```

```python
from contextlib import ExitStack

import numpy as np
import concourse.bass as bass
from concourse import mybir

F32 = mybir.dt.float32
I32 = mybir.dt.int32
ALU = mybir.AluOpType
ACT = mybir.ActivationFunctionType
AX = mybir.AxisListType.X

P = 128
D = 1024
S = 512
T = S // P
C = D // P
EPS = 1e-6
GQ, GK, GV, GG, GA, FU, CQ, CKV, KR, W_IN = 0, 128, 256, 512, 768, 800, 1056, 1312, 1440, 1472
GH, GDK, GDV, TAU, CHUNK = 4, 32, 64, 16.0, 64
NCH = S // CHUNK
MH, NOPE, ROPE, MV = 8, 64, 32, 64
QD = NOPE + ROPE
HALF = ROPE // 2
NG, EPG, NE, DE = 4, 8, 32, 256
BLOCK = 64
RING = 4
FIRST = RING + 2
TURNS = (NE - FIRST) // RING
GATHERED = (2, 3, 4)
OVB = S // BLOCK
STACK, ONE_UP, SMALL = 65, 65 + NG + NE, 65 + NG + NE + BLOCK
EMPTY = 4096.0
NBIG = -1.0e30
MAGIC = 12582912.0
TWO_PI_PARTS = (6.28125, 0.0019350051879882812, 3.019916e-07, -1.9551e-11)


def psum_plan():
    plan, fills, frees = {}, [0] * 8, [0] * 8

    def use(key, bank, readers=1, fill=1):
        fills[bank] += fill
        before = frees[bank]
        frees[bank] += readers
        plan[key] = (bank, fills[bank], before, frees[bank])

    turn = [0]

    def ring(key, readers=1):
        use(key, turn[0] % 8, readers)
        turn[0] += 1

    for c in range(C):
        ring(("xT", c))
    for i in range(3):
        ring(("pT", i))
    for t in range(T):
        ring(("ckr", t))
        ring(("ucq", t))
        if t == 0:
            ring(("z", 0))
            ring(("z", 1))
    for t in range(T):
        ring(("vg", t))
    ring("ckvT")
    for c in range(2):
        ring(("cqT", c))
    ring("krT")
    for h in range(MH):
        ring(("kT", h))
    for t in range(T):
        ring(("V", t))
    for t in range(T):
        for n in range(2):
            ring(("q", t, n))
    for i in range(4):
        ring(("AB", i))
    ring("M")
    for t in range(T):
        ring(("fy", t))
    for d in range(2):
        ring(("kendT", d))
    for d in range(2):
        ring(("kv", d, 0))
        ring(("kv", d, 1))
    for tp in range(2):
        for h in range(GH):
            ring(("att", tp, h))
    for h in range(GH):
        ring(("o", h))
    for h in range(MH):
        ring(("qT", h))
    for i in range(T * MH + 2):
        if i < T * MH:
            use(("S", i), i % 3)
        if i >= 2:
            j = i - 2
            if j % MH == 0:
                use(("O", j // MH), 6 + j // MH % 2, fill=0)
            use(("PT", j), 3 + j % 3)
    turn[0] = 0
    for c in range(C):
        ring(("mT", c))
    turn[0] = 0

    def late(key):
        use(key, 2 + turn[0] % 6)
        turn[0] += 1

    for step in OUT_ORDER:
        if step[0] == "T":
            late(("x2T", step[1], 0))
            late(("x2T", step[1], 1))
        elif step[0] != "pick":
            late(step)
    late("count")
    late("listT")
    return plan, fills, frees


OUT_ORDER = [("out", 0, 0), ("out", 0, 1), ("out", 1, 0), ("T", 0), ("out", 1, 1), ("Lf", 0), ("out", 2, 0),
             ("L", 0), ("T", 1), ("out", 2, 1), ("pos", 0), ("Lf", 1), ("out", 3, 0), ("L", 1), ("T", 2),
             ("Lf", 2), ("L", 2), ("out", 3, 1), ("pick", 0), ("pos", 1), ("T", 3), ("pos", 2), ("Lf", 3), ("L", 3),
             ("pick", 1), ("pick", 2), ("pos", 3), ("pick", 3)]


def picked(pair):
    return pair not in GATHERED


def picks(pair):
    return sum(picked(q) for q in range(pair + 1))


def shape_constants():
    k = np.arange(S)
    ang = 2.0 * np.pi * ((k[:, None] * k[None, :]) % S) / S
    dft = np.stack([np.cos(ang), np.sin(ang)]) / np.sqrt(S)
    k = np.arange(64)
    ang = 2.0 * np.pi * ((k[:, None] * k[None, :]) % 64) / 64
    chan = np.zeros((P, 2, P))
    for g in range(2):
        chan[g * 64:g * 64 + 64, 0, g * 64:g * 64 + 64] = np.cos(ang) / 8.0
        chan[g * 64:g * 64 + 64, 1, g * 64:g * 64 + 64] = -np.sin(ang) / 8.0
    j, i = np.arange(P)[:, None], np.arange(P)[None, :]
    same = j // CHUNK == i // CHUNK
    mask = np.stack([same & (j <= i), same & (j > i)], axis=1)
    tri = np.stack([j < i, np.ones((P, P), bool)], axis=1)
    small = np.zeros((P, SMALL))
    small[:, ONE_UP:] = np.arange(BLOCK) + 1
    small[:, 0:32] = np.arange(NE) * S
    small[:, STACK:ONE_UP] = np.arange(P)[:, None] % 64 == np.arange(NG + NE)[None, :]
    small[:, 40] = np.arange(P) // BLOCK
    for t in range(T):
        for r in range(2):
            small[:, 41 + 2 * t + r] = r * S + t * P + np.arange(P)
    inv = (1.0 / (np.float32(10000.0) ** (np.arange(0, ROPE, 2, dtype=np.float32) / np.float32(ROPE))))
    small[:, 49:65] = inv.astype(np.float32)
    f = np.float32
    rank = np.tile(np.arange(NE) - 100.0, (P, 1))
    return {"c_rank": rank.astype(f), "c_ident": np.eye(P, dtype=f), "c_dft": dft.astype(f), "c_chan": chan.astype(f),
            "c_mask": mask.astype(np.int32), "c_tri": tri.astype(f), "c_small": small.astype(f)}


def encoder_kernel(nc, d, out):
    ctx = ExitStack()
    with ctx:
        def sb(name, shape, dt=F32):
            return ctx.enter_context(nc.sbuf_tensor(name, shape, dt))

        def sem(name):
            return ctx.enter_context(nc.semaphore(name))

        PLAN, FILLS, FREES = psum_plan()

        x_v = d["x"].rearrange("b (t p) n -> p (b t) n", p=P)
        out_v = out.rearrange("b (t p) n -> p (b t) n", p=P)
        w_in_v = d["w_in"][0].rearrange("(p c) n -> p c n", c=C)
        w_out_v = d["w_out"][0].rearrange("(p c) n -> p c n", c=C)
        w_gate_v = d["moe_w_gate"][0].rearrange("e (p c) n -> e p (c n)", c=C)
        w_up_v = d["moe_w_up"][0].rearrange("e (p c) n -> e p (c n)", c=C)
        w_down_v = d["moe_w_down"][0].rearrange("e (c p) n -> e p c n", c=2)
        x2_d = nc.dram_tensor("x2_scratch", (S, D), F32, kind="Internal").ap()
        list_d = nc.dram_tensor("list_scratch", (NE * S, 1), F32, kind="Internal").ap()
        y_d = nc.dram_tensor("y_scratch", (2 * S, D), F32, kind="Internal").ap()
        x2_rows = x2_d.rearrange("t (h n) -> (t h) n", h=2)
        y_rows = y_d.rearrange("t (h n) -> (t h) n", h=2)

        X = sb("X", [P, T, D])
        MIX = sb("MIX", [P, T, D])
        XT = sb("XT", [P, C * S])
        WO = sb("WO", [P, C * D])
        EW = sb("EW", [P, RING, 3, C * DE])
        G = sb("G", [P, 5632])
        ident = sb("ident", [P, P])
        mask = sb("mask", [P, 2, P], I32)
        tri = sb("tri", [P, 2, P])
        small = sb("small", [P, SMALL])
        pos1 = sb("pos1", [P, T, NE])
        rank = sb("rank", [P, NE])
        wr = sb("wr", [P, C, 64])
        rbias = sb("rbias", [P, NG + NE])
        gain1 = sb("gain1", [P, C])
        gainq = sb("gainq", [P, 2])
        gainkv = sb("gainkv", [P, 1])
        gain_gla = sb("gain_gla", [P, GDV])
        ba = sb("ba", [P, 2])
        stat = sb("stat", [P, 64])
        ropet = sb("ropet", [P, 2, T, HALF])
        wts = sb("wts", [P, T, 2])
        gidx = sb("gidx", [P, NE], I32)
        sidx = sb("sidx", [P, NE], I32)
        dest = sb("dest", [P, T, 2], I32)
        nmax = sb("nmax", [P, 1], I32)

        def view(region, start, shape):
            n = 1
            for s in shape:
                n *= s
            ap = region[:, start:start + n]
            if len(shape) == 1:
                return ap
            names = "abcd"[:len(shape)]
            return ap.rearrange(f"p ({' '.join(names)}) -> p {' '.join(names)}",
                                **{k: s for k, s in zip(names[1:], shape[1:])})

        xnT = view(XT, 0, (C, S))
        att = view(XT, 0, (T, GH, P))
        kend_tok = view(XT, 2048, (2, T, P))
        state = view(XT, 3072, (2, NCH, GDV))
        wof = WO[:, :]
        dft = view(WO, 0, (2, T, S))
        AB = view(WO, 4096, (2, 2, S))
        gexp = view(WO, 6144, (2, 2, S))
        osq = view(WO, 6144, (GH, T, GDV))
        w_out_sb = view(WO, 0, (C, D))
        ew01 = EW[:, 0:2].rearrange("p r w n -> p (r w n)")
        ew23 = EW[:, 2:4].rearrange("p r w n -> p (r w n)")
        w_in_sb = view(ew01, 0, (C, W_IN))
        qT = view(ew01, 0, (MH, S))
        kT = view(ew01, 4096, (MH, S))
        V = view(ew01, 8192, (T, MH * MV))
        probs = view(ew01, 10240, (2, S))
        probsT = view(ew01, 11264, (2, S))
        fw = view(ew01, 10240, (2, P))
        chan = view(ew01, 10496, (2, P))
        fM = view(ew01, 10752, (2, 2, P))
        rtmp = view(ew01, 11264, (4, MH, HALF))
        ucq = view(ew23, 0, (T, 512))
        vg = view(ew23, 2048, (T, 512))
        ckr = view(ew23, 4096, (T, 160))
        krp = view(ew23, 4736, (T, QD))
        w_uq = view(ew23, 5120, (2, MH * QD))
        w_ukv = view(ew23, 6656, (MH, NOPE + MV))
        cqT = view(ew23, 7680, (2, S))
        ckvT = view(ew23, 8704, (S,))
        qs = view(ew23, 9216, (T, MH, QD))
        qg = view(G, 0, (S,))
        kg = view(G, 512, (S,))
        la = view(G, 1024, (2, S))
        cum = view(G, 2048, (2, S))
        qdec = view(G, 3072, (2, S))
        kinv = view(G, 4096, (2, S))
        keep = view(G, 5120, (S,))
        gaT = ew23[0:32, 9600:10112]
        wa = ew23[0:32, 10112:10368].rearrange("p (a n) -> p a n", a=2)
        squares_out = view(ew23, 9216, (256,))
        sgt = view(ew01, 0, (T, 256))
        posi = sb("posi", [P, T], I32)
        posf = sb("posf", [P, T])
        rgla = sb("rgla", [P, 4, GH * T])
        nm = sb("nm", [P, T * MH])
        rs = sb("rs", [P, T * MH])
        ri = sb("ri", [P, T * MH])
        lfill = sb("lfill", [P, P])
        held = sb("held", [P, 2])
        g2b = view(G, 4608, (D,))
        sqj = view(G, 3584, (D,))
        tot = sb("tot", [P, 2, NCH])
        dec = sb("dec", [P, 2, NCH])
        xeT = view(WO, 6144, (2, C, P))
        sel = view(G, 4608, (2, T, 2, BLOCK))
        sel0 = view(G, 2560, (T, 2, BLOCK))
        Y = view(G, 2560, (2, 512))
        hs = view(G, 3584, (2, P))
        hg = view(G, 3840, (2, P))
        hT = view(G, 4096, (2, 2, BLOCK))
        gfb = view(XT, 0, (D,))
        xg = [G[:, 2048:2560], G[:, 4608:5120]]
        gu_at = [EW[:, s, 0:2].rearrange("p w n -> p (w n)") for s in range(RING)]
        gu_at += [WO[:, 0:2 * C * DE], XT[:, 0:2 * C * DE]]
        dn_at = [EW[:, s, 2] for s in range(RING)] + [WO[:, 2 * C * DE:3 * C * DE], G[:, 0:C * DE]]
        lg = view(G, 0, (T, NG + NE))
        rt = view(G, 160, (T, 14, NE))
        mska = view(G, 2048, (T, NE))
        oh = view(G, 2176, (T, 2, NE))
        lst = G[0:NE, 2432:2560]
        rn2 = view(G, 3080, (T, 8))
        lv = view(G, 4352, (3, NE))
        lf = view(G, 3120, (2, P))
        ovl = view(G, 4448, (4,))
        ov_g = sb("ov_g", [P, 1], I32)
        ov_s = sb("ov_s", [P, 1], I32)
        junk = XT
        ywide = EW[:, :].rearrange("p r w n -> p (r w n)")
        ypair = view(ywide, 0, (T, 2, D))

        banks = [ctx.enter_context(nc.psum_tensor(f"bank{b}", [P, 512], F32)) for b in range(8)]

        bank_full = [sem(f"bank_full{b}") for b in range(8)]
        bank_free = [sem(f"bank_free{b}") for b in range(8)]
        x_landed = [sem(f"x_landed{t}") for t in range(T)]
        win_landed = [sem(f"win_landed{i}") for i in range(3)]
        first_landed = sem("first_landed")
        consts_landed = sem("consts_landed")
        gate_w_landed = sem("gate_w_landed")
        mla_w_landed = sem("mla_w_landed")
        dft_landed = sem("dft_landed")
        fnet_landed = sem("fnet_landed")
        wout_landed = sem("wout_landed")
        gf_landed = sem("gf_landed")
        krope_copied = sem("krope_copied")
        dve_chain = sem("dve_chain")
        act_chain = sem("act_chain")
        pool_chain = sem("pool_chain")
        angles_ready = sem("angles_ready")
        tables_ready = sem("tables_ready")
        squares_ready = sem("squares_ready")
        var_ready = sem("var_ready")
        guess_ready = sem("guess_ready")
        xn_ready = sem("xn_ready")
        gate_abs = sem("gate_abs")
        gate_log = sem("gate_log")
        decay_sum = sem("decay_sum")
        decay_exp = sem("decay_exp")
        gla_ready = sem("gla_ready")
        silu_exp = sem("silu_exp")
        latents_ready = sem("latents_ready")
        kr_raw = sem("kr_raw")
        kr_rot = sem("kr_rot")
        q_rot = sem("q_rot")
        gatew_zero = sem("gatew_zero")
        fnetw_zero = sem("fnetw_zero")
        att_zero = sem("att_zero")
        gla_out = sem("gla_out")
        keep_ready = sem("keep_ready")
        av_done = sem("av_done")
        g2_landed = sem("g2_landed")
        x3_ready = sem("x3_ready")
        ov_tmp = sem("ov_tmp")
        held_done = sem("held_done")
        SQ2, SQ3 = T + 2 * T + GH, 3 * T + 2 * T + GH
        neg_max = sem("neg_max")
        x2_ready = sem("x2_ready")
        x2_stored = sem("x2_stored")
        logit_ready = sem("logit_ready")
        rexp_ready = sem("rexp_ready")
        picks_ready = sem("picks_ready")
        dest_ready = sem("dest_ready")
        list_filled = sem("list_filled")
        fill_ready = sem("fill_ready")
        scattered = sem("scattered")
        list_loaded = sem("list_loaded")
        idx_ready = sem("idx_ready")
        nmax_ready = sem("nmax_ready")
        xg_landed = [sem(f"xg_landed{s}") for s in range(2)]
        sel_ready = sem("sel_ready")
        gu_landed = [sem(f"gu_landed{s}") for s in range(FIRST)]
        dn_landed = [sem(f"dn_landed{s}") for s in range(FIRST)]
        xe_full = sem("xe_full")
        xe_ready = sem("xe_ready")
        gu_full = sem("gu_full")
        silu_done = sem("silu_done")
        hg_ready = sem("hg_ready")
        hT_full = sem("hT_full")
        hT_ready = sem("hT_ready")
        y_full = sem("y_full")
        y_ready = sem("y_ready")
        y_stored = [sem(f"y_stored{s}") for s in range(2)]
        ov_w = sem("ov_w")
        ov_list = sem("ov_list")
        ov_idx = sem("ov_idx")
        ov_x = sem("ov_x")
        ov_xt = sem("ov_xt")
        ov_xc = sem("ov_xc")
        ov_gu = sem("ov_gu")
        ov_silu = sem("ov_silu")
        ov_hg = sem("ov_hg")
        ov_hT = sem("ov_hT")
        ov_hc = sem("ov_hc")
        ov_y = sem("ov_y")
        ov_yc = sem("ov_yc")
        ov_stored = sem("ov_stored")
        moe_done = sem("moe_done")
        pair_landed = [[sem(f"pair_landed{t}_{r}") for r in range(2)] for t in range(T)]
        x3_gain = sem("x3_gain")
        root_ready = sem("root_ready")
        out_ready = sem("out_ready")
        out_stored = sem("out_stored")

        def open_bank(key):
            b, _, before, _ = PLAN[key]
            if before:
                nc.tensor.wait_ge(bank_free[b], before)
            return banks[b]

        def close_bank(ins, key):
            ins.then_inc(bank_full[PLAN[key][0]], 1)

        def filled(eng, key):
            b, full, _, _ = PLAN[key]
            eng.wait_ge(bank_full[b], full)
            return banks[b]

        def free_bank(ins, key):
            ins.then_inc(bank_free[PLAN[key][0]], 1)

        def drained(eng, key):
            b, _, _, after = PLAN[key]
            eng.wait_ge(bank_free[b], after)

        def linker(eng, chain):
            count = [0]

            def link(ins):
                count[0] += 1
                ins.then_inc(chain, 1)
                eng.wait_ge(chain, count[0])
            return link

        N_CONSTS = 12
        block = ctx.enter_context(nc.Block())

        @block.sync
        def _(sp):
            sp.dma_start(small[:, :], d["c_small"]).then_inc(first_landed, 16)
            sp.dma_start(posi[:, :],
                         d["positions"].rearrange("b (t p) -> p (b t)", p=P),
                         allow_slow_non_contiguous=True).then_inc(first_landed, 16)
            sp.dma_start(ident[:, :], d["c_ident"]).then_inc(first_landed, 16)
            sp.dma_start(gain1[:, :], d["norm1_g"][0].rearrange("(p c) -> p c", c=C)).then_inc(first_landed, 16)
            for t in range(T):
                sp.dma_start(X[:, t, :], x_v[:, t, :]).then_inc(x_landed[t], 16)
            sp.dma_start(w_in_sb[:, :, GA:W_IN], w_in_v[:, :, GA:W_IN]).then_inc(win_landed[0], 16)
            sp.dma_start(w_in_sb[:, :, GQ:GV], w_in_v[:, :, GQ:GV]).then_inc(win_landed[1], 16)
            sp.dma_start(w_in_sb[:, :, GV:GA], w_in_v[:, :, GV:GA]).then_inc(win_landed[2], 16)
            sp.wait_ge(gatew_zero, 2)
            sp.dma_start(wa[0:16, 0, :], d["gla_wa_f"][0]).then_inc(gate_w_landed, 16)
            sp.dma_start(wa[16:32, 1, :], d["gla_wa_b"][0]).then_inc(gate_w_landed, 16)
            for dst, src in ((ba[:, 0:1], d["gla_ba_f"].rearrange("l n -> n l")),
                             (ba[:, 1:2], d["gla_ba_b"].rearrange("l n -> n l")),
                             (gainq[:, :], d["mla_q_norm_g"][0].rearrange("(p c) -> p c", c=2)),
                             (gainkv[:, :], d["mla_kv_norm_g"].rearrange("l n -> n l")),
                             (gain_gla[:, :], d["gla_norm_g"][0].partition_broadcast(P)),
                             (mask[:, :, :], d["c_mask"]),
                             (tri[:, :, :], d["c_tri"]),
                             (rank[:, :], d["c_rank"]),
                             (wr[:, :, 0:NG], d["moe_w_rg"][0].rearrange("(p c) n -> p c n", c=C)),
                             (wr[:, :, NG:NG + NE], d["moe_w_re"][0].rearrange("(p c) n -> p c n", c=C)),
                             (rbias[:, 0:NG], d["moe_b_rg"][0].partition_broadcast(P)),
                             (rbias[:, NG:], d["moe_b_re"][0].partition_broadcast(P))):
                sp.dma_start(dst, src).then_inc(consts_landed, 16)
            sp.dma_start(w_uq, d["mla_w_uq"][0].rearrange("(p c) n -> p c n", c=2)).then_inc(mla_w_landed, 16)
            sp.dma_start(w_ukv.rearrange("p a b -> p (a b)"), d["mla_w_ukv"][0]).then_inc(mla_w_landed, 16)
            for i in range(2):
                sp.dma_start(dft[:, i], d["c_dft"][i].rearrange("(t p) n -> p t n", p=P)).then_inc(dft_landed, 16)
            sp.wait_ge(fill_ready, 1)
            sp.dma_start(list_d.rearrange("(p n) o -> p (n o)", p=P), lfill[:, :]).then_inc(list_filled, 16)
            sp.wait_ge(fnetw_zero, 1)
            for g in range(4):
                r = slice(64 * (g % 2), 64 * (g % 2) + 64)
                sp.dma_start(fw[r, g // 2, r], d["fnet_w"][0, g]).then_inc(fnet_landed, 16)
            sp.dma_start(chan, d["c_chan"]).then_inc(fnet_landed, 16)
            drained(sp, "krT")
            for h in range(1, MH):
                sp.dma_start(kT[NOPE:QD, h, :], kT[NOPE:QD, 0, :]).then_inc(krope_copied, 16)
            drained(sp, ("fy", T - 1))
            sp.wait_ge(gla_out, 1)
            sp.dma_start(g2b, d["norm2_g"][0].partition_broadcast(P)).then_inc(g2_landed, 16)
            sp.dma_start(WO[:, 0:C * D // 2], w_out_v[:, 0:C // 2].rearrange("p c n -> p (c n)")).then_inc(wout_landed, 16)
            sp.dma_start(WO[:, C * D // 2:], w_out_v[:, C // 2:].rearrange("p c n -> p (c n)")).then_inc(wout_landed, 16)

            def load_gate_up(place, e):
                one = isinstance(e, int)
                for w, src in enumerate((w_gate_v, w_up_v)):
                    sp.dma_start(gu_at[place][:, w * C * DE:(w + 1) * C * DE],
                                 src[e] if one else src[e].rearrange("e p n -> p (e n)")).then_inc(gu_landed[place], 16)

            def load_down(place, e):
                one = isinstance(e, int)
                sp.dma_start(dn_at[place].rearrange("p (c n) -> p c n", c=2),
                             w_down_v[e] if one else w_down_v[e].rearrange("e p c n -> p (e c) n")).then_inc(dn_landed[place], 16)

            for h in range(MH):
                drained(sp, ("qT", h))
            for s in (2, 3):
                load_gate_up(s, s)
                load_down(s, s)
            for t in range(T):
                drained(sp, ("O", t))
            for s in (0, 1):
                load_gate_up(s, s)
                load_down(s, s)
            for t in range(T):
                if t == T - 1:
                    for u in range(T):
                        for n in range(2):
                            drained(sp, ("out", u, n))
                    load_gate_up(RING, RING)
                    load_down(RING, RING)
                sp.wait_ge(x2_ready, t + 1)
                sp.dma_start(x2_d[t * P:(t + 1) * P, :], MIX[:, t, :]).then_inc(x2_stored, 16)
            for t in range(T):
                drained(sp, ("Lf", t))
            load_gate_up(RING + 1, RING + 1)
            sp.wait_ge(scattered, 16 * 2 * T)
            for i in range(2):
                sp.dma_start(lst[:, i * BLOCK:(i + 1) * BLOCK],
                             list_d.rearrange("(e s) o -> e (s o)", e=NE)[:, 0:BLOCK]).then_inc(list_loaded, 16)
            sp.wait_ge(idx_ready, 1)
            load_down(RING + 1, RING + 1)
            for s in range(RING):
                sp.wait_ge(gu_full, s + 1)
                load_gate_up(s, FIRST + s)
                sp.wait_ge(y_full, s + 1)
                load_down(s, FIRST + s)
            with sp.Fori(1, TURNS) as i:
                for s in range(RING):
                    e = i * RING + (FIRST + s)
                    sp.wait_ge(gu_full, i * RING + (FIRST + s - RING + 1))
                    load_gate_up(s, bass.ds(e, 1))
                    sp.wait_ge(y_full, i * RING + (FIRST + s - RING + 1))
                    load_down(s, bass.ds(e, 1))
            for e in range(FIRST + TURNS * RING, NE):
                sp.wait_ge(gu_full, e - RING + 1)
                load_gate_up((e - FIRST) % RING, e)
                sp.wait_ge(y_full, e - RING + 1)
                load_down((e - FIRST) % RING, e)
            sp.dma_start(gfb, d["final_norm_g"].partition_broadcast(P)).then_inc(gf_landed, 16)
            sp.wait_ge(nmax_ready, 1)
            sp.wait_ge(y_full, NE)
            with sp.If(sp.value_load(nmax[0:1, 0:1]) > BLOCK):
                with sp.Fori(0, NE) as e:
                    with sp.Fori(0, OVB) as k:
                        for q in range(2):
                            sp.wait_ge(held_done, e * (OVB * 3) + k * 3 + 1)
                            sp.dma_start(ovl[q * BLOCK:(q + 1) * BLOCK, 0:1],
                                         list_d[bass.ds(e * S + k * BLOCK, BLOCK), :]).then_inc(ov_list, 16)
                        for w, src in enumerate((w_gate_v, w_up_v)):
                            sp.wait_ge(ov_y, e * OVB + k + 1)
                            sp.dma_start(EW[:, 0, w], src[bass.ds(e, 1)].rearrange("e p n -> p (e n)")).then_inc(ov_w, 16)
                        sp.dma_start(EW[:, 0, 2].rearrange("p (c n) -> p c n", c=2),
                                     w_down_v[bass.ds(e, 1)].rearrange("e p c n -> p (e c) n")).then_inc(ov_w, 16)
            sp.wait_ge(moe_done, 1)
            for t in range(T):
                for r in range(2):
                    sp.dma_start(ypair[:, t, r], y_d[r * S + t * P:r * S + (t + 1) * P, :]).then_inc(pair_landed[t][r], 16)
            for t in range(T):
                sp.wait_ge(out_ready, t + 1)
                sp.dma_start(out_v[:, t, :], X[:, t, :]).then_inc(out_stored, 16)
            sp.wait_ge(out_stored, 16 * T)

        @block.tensor
        def _(pe):
            pe.wait_ge(first_landed, 64)
            pe.wait_ge(xn_ready, T)
            for c in range(C):
                ps = open_bank(("xT", c))
                for t in range(T):
                    mm = pe.transpose(ps[:, t * P:(t + 1) * P], MIX[:, t, c:D:C], ident[:, :])
                close_bank(mm, ("xT", c))
            for c in range(C):
                drained(pe, ("xT", c))

            def by_feature(key, col, width):
                ps = open_bank(key)
                for c in range(C):
                    mm = pe.matmul(ps[0:width, :], w_in_sb[:, c, col:col + width], xnT[:, c, :],
                                   start=(c == 0), stop=(c == C - 1))
                close_bank(mm, key)

            def by_token(key, t, col, width):
                ps = open_bank(key)
                for c in range(C):
                    mm = pe.matmul(ps[:, 0:width], xnT[:, c, t * P:(t + 1) * P], w_in_sb[:, c, col:col + width],
                                   start=(c == 0), stop=(c == C - 1))
                close_bank(mm, key)

            pe.wait_ge(win_landed[0], 16)
            by_feature(("pT", 0), GA, 32)
            pe.wait_ge(win_landed[1], 16)
            by_feature(("pT", 1), GQ, 128)
            by_feature(("pT", 2), GK, 128)
            for t in range(T):
                by_token(("ckr", t), t, CKV, 160)
                by_token(("ucq", t), t, FU, 512)
                if t == 0:
                    pe.wait_ge(gate_w_landed, 32)
                    drained(pe, ("pT", 0))
                    for dd in range(2):
                        ps = open_bank(("z", dd))
                        close_bank(pe.matmul(ps[:, :], wa[:, dd, :], gaT[:, :], start=True, stop=True), ("z", dd))
            pe.wait_ge(win_landed[2], 16)
            for t in range(T):
                by_token(("vg", t), t, GV, 512)

            pe.wait_ge(latents_ready, 8)
            ps = open_bank("ckvT")
            for t in range(T):
                mm = pe.transpose(ps[:, t * P:(t + 1) * P], ckr[:, t, 0:128], ident[:, :])
            close_bank(mm, "ckvT")
            for c in range(2):
                ps = open_bank(("cqT", c))
                for t in range(T):
                    mm = pe.transpose(ps[:, t * P:(t + 1) * P], ucq[:, t, 256 + c:512:2], ident[:, :])
                close_bank(mm, ("cqT", c))
            pe.wait_ge(kr_rot, 1)
            ps = open_bank("krT")
            for t in range(T):
                mm = pe.transpose(ps[0:QD, t * P:(t + 1) * P], krp[:, t, :], ident[:, :])
            close_bank(mm, "krT")
            drained(pe, "ckvT")
            pe.wait_ge(mla_w_landed, 32)
            for h in range(MH):
                ps = open_bank(("kT", h))
                close_bank(pe.matmul(ps[0:NOPE, :], w_ukv[:, h, 0:NOPE], ckvT, start=True, stop=True), ("kT", h))
            for t in range(T):
                ps = open_bank(("V", t))
                close_bank(pe.matmul(ps[:, :], ckvT[:, t * P:(t + 1) * P], w_ukv[:, :, NOPE:],
                                     start=True, stop=True), ("V", t))
            drained(pe, ("cqT", 0))
            drained(pe, ("cqT", 1))
            for t in range(T):
                for n in range(2):
                    ps = open_bank(("q", t, n))
                    for c in range(2):
                        mm = pe.matmul(ps[:, 0:384], cqT[:, c, t * P:(t + 1) * P], w_uq[:, c, n * 384:(n + 1) * 384],
                                       start=(c == 0), stop=(c == 1))
                    close_bank(mm, ("q", t, n))

            pe.wait_ge(dft_landed, 32)
            for i in range(4):
                ps = open_bank(("AB", i))
                for t in range(T):
                    mm = pe.matmul(ps[:, :], ucq[:, t, (i % 2) * P:(i % 2 + 1) * P], dft[:, i // 2, t, :],
                                   start=(t == 0), stop=(t == T - 1))
                close_bank(mm, ("AB", i))
            pe.wait_ge(fnet_landed, 80)
            ps = open_bank("M")
            for i in range(2):
                for blk in range(2):
                    at = (2 * i + blk) * P
                    mm = pe.matmul(ps[:, at:at + P], chan[:, i, :], fw[:, blk, :], start=True, stop=True)
            close_bank(mm, "M")
            for i in range(4):
                drained(pe, ("AB", i))
            drained(pe, "M")
            for t in range(T):
                ps = open_bank(("fy", t))
                for blk in range(2):
                    for i in range(2):
                        mm = pe.matmul(ps[:, blk * P:(blk + 1) * P], AB[:, i, blk, t * P:(t + 1) * P],
                                       fM[:, i, blk, :], start=(i == 0), stop=(i == 1))
                close_bank(mm, ("fy", t))

            pe.wait_ge(gla_ready, 6)
            for dd in range(2):
                ps = open_bank(("kendT", dd))
                for t in range(T):
                    mm = pe.transpose(ps[:, t * P:(t + 1) * P], gexp[:, dd, 0, t * P:(t + 1) * P], ident[:, :])
                close_bank(mm, ("kendT", dd))
            for dd in range(2):
                drained(pe, ("kendT", dd))
                for odd in range(2):
                    ps = open_bank(("kv", dd, odd))
                    rows = slice(CHUNK * odd, CHUNK * odd + CHUNK)
                    for t in range(T):
                        for h in range(GH):
                            mm = pe.matmul(ps[GDK * h:GDK * (h + 1), t * GDV:(t + 1) * GDV],
                                           kend_tok[rows, dd, t, GDK * h:GDK * (h + 1)],
                                           vg[rows, t, GDV * h:GDV * (h + 1)], start=True, stop=True)
                    close_bank(mm, ("kv", dd, odd))
            for tp in range(2):
                heads = [open_bank(("att", tp, h)) for h in range(GH)]
                for dd in range(2):
                    for u in range(2):
                        t = 2 * tp + u
                        at = (2 * dd + u) * P
                        for h in range(GH):
                            rows = slice(GDK * h, GDK * (h + 1))
                            mm = pe.matmul(heads[h][:, at:at + P], kinv[rows, dd, t * P:(t + 1) * P],
                                           qdec[rows, dd, t * P:(t + 1) * P], start=True, stop=True)
                            if dd == 1 and u == 1:
                                close_bank(mm, ("att", tp, h))
            for dd in range(2):
                drained(pe, ("kv", dd, 0))
                drained(pe, ("kv", dd, 1))
            heads = []
            for h in range(GH):
                for tp in range(2):
                    drained(pe, ("att", tp, h))
                heads.append(open_bank(("o", h)))
                for t in range(T):
                    pe.matmul(heads[h][:, t * GDV:(t + 1) * GDV], att[:, t, h, :], vg[:, t, GDV * h:GDV * (h + 1)],
                              start=(t == 0), stop=False, skip_group_check=True)
            last = [(t, dd, u) for t in range(T) for dd in range(2) for u in range(2)
                    if 2 * t + u != (0 if dd == 0 else NCH - 1)]
            for t, dd, u in last:
                n = 2 * t + u
                for h in range(GH):
                    rows = slice(GDK * h, GDK * (h + 1))
                    mm = pe.matmul(heads[h][CHUNK * u:CHUNK * (u + 1), t * GDV:(t + 1) * GDV],
                                   qdec[rows, dd, n * CHUNK:(n + 1) * CHUNK], state[rows, dd, n, :],
                                   start=False, stop=False, skip_group_check=True)
                    if (t, dd, u) == last[-1]:
                        close_bank(mm, ("o", h))

            pe.wait_ge(q_rot, T)
            for h in range(MH):
                ps = open_bank(("qT", h))
                for t in range(T):
                    mm = pe.transpose(ps[0:QD, t * P:(t + 1) * P], qs[:, t, h, :], ident[:, :])
                close_bank(mm, ("qT", h))
            pe.wait_ge(krope_copied, 16 * (MH - 1))
            for h in range(MH):
                drained(pe, ("kT", h))
                drained(pe, ("qT", h))
            for t in range(T):
                drained(pe, ("V", t))
            for i in range(T * MH + 3):
                if i < T * MH:
                    ps = open_bank(("S", i))
                    tq, h = i // MH, i % MH
                    close_bank(pe.matmul(ps[:, :], qT[0:QD, h, tq * P:(tq + 1) * P], kT[0:QD, h, :],
                                         start=True, stop=True), ("S", i))
                j = i - 2
                if 0 <= j < T * MH:
                    drained(pe, ("S", j))
                    ps = open_bank(("PT", j))
                    for kc in range(T):
                        mm = pe.transpose(ps[:, kc * P:(kc + 1) * P], probs[:, j % 2, kc * P:(kc + 1) * P], ident[:, :])
                    close_bank(mm, ("PT", j))
                j = i - 3
                if j >= 0:
                    tq, h = j // MH, j % MH
                    if h == 0:
                        ps_o = open_bank(("O", tq))
                    drained(pe, ("PT", j))
                    for kc in range(T):
                        mm = pe.matmul(ps_o[:, h * MV:(h + 1) * MV], probsT[:, j % 2, kc * P:(kc + 1) * P],
                                       V[:, kc, h * MV:(h + 1) * MV], start=(kc == 0), stop=(kc == T - 1))
                    mm.then_inc(av_done, 1)

            pe.wait_ge(gla_out, 1)
            for t in range(T):
                drained(pe, ("O", t))
                drained(pe, ("fy", t))
            for c in range(C):
                ps = open_bank(("mT", c))
                for t in range(T):
                    mm = pe.transpose(ps[:, t * P:(t + 1) * P], MIX[:, t, c:D:C], ident[:, :])
                close_bank(mm, ("mT", c))
            for c in range(C):
                drained(pe, ("mT", c))
            pe.wait_ge(wout_landed, 32)
            pe.wait_ge(consts_landed, 16 * N_CONSTS)
            for step in OUT_ORDER:
                kind, t = step[0:2]
                if kind == "out":
                    n = step[2]
                    ps = open_bank(step)
                    for c in range(C):
                        mm = pe.matmul(ps[:, :], xnT[:, c, t * P:(t + 1) * P], w_out_sb[:, c, n * 512:(n + 1) * 512],
                                       start=(c == 0), stop=(c == C - 1))
                    close_bank(mm, step)
                elif kind == "T":
                    pe.wait_ge(x2_ready, t + 1)
                    for q in range(2):
                        ps = open_bank(("x2T", t, q))
                        for j in range(4):
                            c = 4 * q + j
                            mm = pe.transpose(ps[:, j * P:(j + 1) * P], MIX[:, t, c * P:(c + 1) * P], ident[:, :])
                        close_bank(mm, ("x2T", t, q))
                elif kind == "Lf":
                    drained(pe, ("x2T", t, 0))
                    drained(pe, ("x2T", t, 1))
                    ps = open_bank(step)
                    for c in range(C):
                        half = slice(64 * (c % 2), 64 * (c % 2) + 64)
                        mm = pe.matmul(ps[half, 0:P], wr[:, c, :], xnT[:, c, t * P:(t + 1) * P],
                                       start=(c < 2), stop=(c >= C - 2))
                    close_bank(mm, step)
                elif kind == "L":
                    drained(pe, ("Lf", t))
                    ps = open_bank(step)
                    close_bank(pe.matmul(ps[:, 0:NG + NE], lf[:, t % 2], small[:, STACK:ONE_UP], start=True, stop=True), step)
                elif kind == "pick":
                    pe.wait_ge(sel_ready, t + 1)
                    if t == 0:
                        drained(pe, ("mT", 0))
                        drained(pe, ("mT", 1))
                    for c in range(C):
                        mm = pe.matmul(banks[c // 4][:, c % 4 * P:(c % 4 + 1) * P], MIX[:, t, c * P:(c + 1) * P],
                                       sel0[:, t].rearrange("p e s -> p (e s)"), start=(t == 0 and c % 4 == 0),
                                       stop=(t == T - 1 and c % 4 == 3), skip_group_check=True)
                        if t == T - 1 and c % 4 == 3:
                            mm.then_inc(xe_full, 1)
                else:
                    pe.wait_ge(picks_ready, t + 1)
                    ps = open_bank(step)
                    for u in range(t + 1):
                        mm = pe.matmul(ps[:, 0:NE], tri[:, 1 if u < t else 0, :], mska[:, u, :],
                                       start=(u == 0), stop=(u == t))
                    close_bank(mm, step)
            ps = open_bank("count")
            for u in range(T):
                mm = pe.matmul(ps[:, 0:NE], tri[:, 1, :], mska[:, u, :], start=(u == 0), stop=(u == T - 1))
            close_bank(mm, "count")
            def select(half, buf):
                for j in range(4):
                    c = 4 * half + j
                    for t in range(T):
                        mm = pe.matmul(banks[half][:, j * P:(j + 1) * P], MIX[:, t, c * P:(c + 1) * P],
                                       sel[:, buf, t].rearrange("p e s -> p (e s)"), start=(t == 0), stop=(t == T - 1))
                return mm

            def tokens(buf, bank):
                for j in range(4):
                    mm = pe.transpose(banks[bank][:, j * P:(j + 1) * P], xg[buf][:, j * P:(j + 1) * P], ident[:, :])
                return mm

            def gate_up(place, par, buf):
                bank = banks[2 + par]
                wv = gu_at[place].rearrange("p (w c n) -> p w c n", w=2, c=C)
                for c in range(C):
                    for m in range(2):
                        mm = pe.matmul(bank[BLOCK * m:BLOCK * (m + 1), 0:2 * P].rearrange("p (w n) -> p w n", w=2),
                                       xeT[:, buf, c, par * BLOCK:(par + 1) * BLOCK],
                                       wv[:, :, c, m * P:(m + 1) * P], start=(c == 0), stop=(c == C - 1))
                return mm

            def transpose_h(par):
                return pe.transpose(banks[6 + par][:, 0:P], hg[:, par], ident[:, :])

            def down(place, par):
                bank = banks[4 + par]
                wv = dn_at[place].rearrange("p (c n) -> p c n", c=2)
                for m in range(2):
                    for q in range(2):
                        mm = pe.matmul(bank[BLOCK * q:BLOCK * (q + 1), :], hT[:, par, m, :],
                                       wv[:, m, q * 512:(q + 1) * 512], start=(m == 0), stop=(m == 1))
                return mm

            def expert(e, r, pick, turns, place, loads, prev, prev_loads):
                known = isinstance(e, int)
                par = r % 2
                pe.wait_ge(gu_landed[place], loads * 32)
                pe.wait_ge(xe_ready, e + (2 - par))
                if not (known and e < 2):
                    pe.wait_ge(hg_ready, e - 1)
                gate_up(place, par, r // 2).then_inc(gu_full, 1)
                if known and e == 0:
                    pe.wait_ge(list_loaded, 32)
                    ps = open_bank("listT")
                    close_bank(pe.transpose(ps[:, 0:NE], lst, ident[0:NE, 0:NE]), "listT")
                if not (known and e >= NE - 2):
                    pe.wait_ge(xe_ready, e + 1)
                    if pick:
                        pe.wait_ge(sel_ready, turns)
                        select(par, 1 - r // 2).then_inc(xe_full, 1)
                    else:
                        pe.wait_ge(xg_landed[par], turns * 16)
                        tokens(par, par).then_inc(xe_full, 1)
                if not (known and e < 1):
                    last_down(e - 1, prev, prev_loads, 1 - par)
                pe.wait_ge(hg_ready, e + 1)
                if not (known and e < 2):
                    pe.wait_ge(hT_ready, e - 1)
                if known and e == 0:
                    drained(pe, "listT")
                transpose_h(par).then_inc(hT_full, 1)

            def last_down(e, place, loads, par):
                pe.wait_ge(dn_landed[place], loads * 16)
                pe.wait_ge(hT_ready, e + 1)
                if not (isinstance(e, int) and e < 2):
                    pe.wait_ge(y_ready, e - 1)
                down(place, par).then_inc(y_full, 1)

            def place(e):
                return (e, 1) if e < FIRST else ((e - FIRST) % RING, (e - FIRST) // RING + 2)

            def known_expert(e):
                nxt = e // 2 + 1
                expert(e, e % 4, picked(nxt), picks(nxt) + T - 1 if picked(nxt) else nxt + 1 - picks(nxt), *place(e), *place(e - 1))

            drained(pe, "count")
            for t in range(T):
                drained(pe, ("pos", t))
                drained(pe, ("L", t))
            for e in range(FIRST + RING):
                known_expert(e)
            with pe.Fori(1, TURNS) as i:
                for s in range(RING):
                    e = FIRST + s
                    expert(i * RING + e, e % 4, True, i * (RING // 2) + (picks(e // 2 + 1) + T - 1),
                           s, i + 2, (s - 1) % RING, i + (2 if s else 1))
            for e in range(FIRST + TURNS * RING, NE):
                known_expert(e)
            last_down(NE - 1, *place(NE - 1), (NE - 1) % 2)

            pe.wait_ge(nmax_ready, 1)
            pe.wait_ge(y_ready, NE)
            with pe.If(pe.value_load(nmax[0:1, 0:1]) > BLOCK):
                pe.nop().then_inc(ov_y, 1)
                with pe.Fori(0, NE * OVB) as n:
                    pe.wait_ge(ov_x, n * 16 + 16)
                    tokens(0, 0).then_inc(ov_xt, 1)
                    pe.wait_ge(ov_w, n * 48 + 48)
                    pe.wait_ge(ov_xc, n + 1)
                    gate_up(0, 0, 0).then_inc(ov_gu, 1)
                    pe.wait_ge(ov_hg, n + 1)
                    transpose_h(0).then_inc(ov_hT, 1)
                    pe.wait_ge(ov_hc, n + 1)
                    down(0, 0).then_inc(ov_y, 1)

        @block.scalar
        def _(act):
            link = linker(act, act_chain)
            norms = [0]

            def root_guess(dst, src):
                norms[0] += 1
                act.wait_ge(var_ready, norms[0])
                link(act.activation(dst, src, ACT.Ln))
                act.activation(dst, dst, ACT.Exp, scale=-0.5).then_inc(guess_ready, 1)

            act.preload_act_table_set("silu_and_others")
            act.wait_ge(angles_ready, 1)
            act.activation(ropet[:, 0], ropet[:, 0], ACT.Sin).then_inc(tables_ready, 1)
            act.activation(ropet[:, 1], ropet[:, 1], ACT.Sin).then_inc(tables_ready, 1)
            for t in range(T):
                act.wait_ge(x_landed[t], 16)
                act.activation(junk[:, 0:D], X[:, t, :], ACT.Square, accum_out=stat[:, t:t + 1]).then_inc(squares_ready, 1)
                act.wait_ge(squares_ready, t + 1)
            act.preload_act_table_set("natural_log_exp_and_others")
            root_guess(stat[:, 8:12], stat[:, 4:8])
            for c in range(0, C, 2):
                ps = filled(act, ("xT", c))
                free_bank(act.activation(xnT[:, c, :], ps[:, :], ACT.Copy, scale=gain1[:, c:c + 1]), ("xT", c))
            ps = filled(act, ("pT", 0))
            free_bank(act.activation(gaT[:, :], ps[0:32, :], ACT.Copy), ("pT", 0))

            def copy_ckr(t):
                ps = filled(act, ("ckr", t))
                free_bank(act.activation(ckr[:, t, :], ps[:, 0:160], ACT.Copy), ("ckr", t))
                drained(act, ("ckr", t))
                act.activation(squares_out[:, 0:128], ckr[:, t, 0:128], ACT.Square, accum_out=stat[:, 20 + t:21 + t]).then_inc(squares_ready, 1)
                act.wait_ge(squares_ready, T + 2 * t + 1)
                drained(act, ("ucq", t))
                act.activation(squares_out, ucq[:, t, 256:512], ACT.Square, accum_out=stat[:, 16 + t:17 + t]).then_inc(squares_ready, 1)
                act.wait_ge(squares_ready, T + 2 * t + 2)

            copy_ckr(0)
            for dd in range(2):
                act.wait_ge(gate_abs, dd + 1)
                link(act.activation(gexp[:, dd, 0], gexp[:, dd, 0], ACT.Exp))
                act.activation(gexp[:, dd, 1], gexp[:, dd, 0], ACT.Ln, bias=1.0).then_inc(gate_log, 1)
            copy_ckr(1)
            for dd in range(2):
                act.wait_ge(decay_sum, dd + 1)
                act.activation(gexp[:, dd, 0], cum[:, dd], ACT.Exp, scale=1.0 / TAU).then_inc(decay_exp, 1)
                act.activation(gexp[:, dd, 1], cum[:, dd], ACT.Exp, scale=-1.0 / TAU).then_inc(decay_exp, 1)
                act.activation(dec[:, dd], tot[:, dd], ACT.Exp, scale=1.0 / TAU).then_inc(decay_exp, 1)
            copy_ckr(2)
            copy_ckr(3)
            root_guess(stat[:, 32:40], stat[:, 24:32])
            for t in range(T):
                ps = filled(act, ("vg", t))
                free_bank(act.activation(vg[:, t, :], ps[:, :], ACT.Copy), ("vg", t))
            for t in range(T):
                drained(act, ("vg", t))
            act.activation(sgt, vg[:, :, 256:512], ACT.Exp, scale=-1.0).then_inc(silu_exp, 1)
            ps = filled(act, "ckvT")
            act.wait_ge(consts_landed, 16 * N_CONSTS)
            free_bank(act.activation(ckvT, ps[:, :], ACT.Copy, scale=gainkv[:, 0:1]), "ckvT")
            ps = filled(act, "krT")
            free_bank(act.activation(kT[NOPE:QD, 0, :], ps[NOPE:QD, :], ACT.Copy), "krT")
            for h in range(0, MH, 2):
                ps = filled(act, ("kT", h))
                free_bank(act.activation(kT[0:NOPE, h, :], ps[0:NOPE, :], ACT.Copy), ("kT", h))
            for t in range(0, T, 2):
                ps = filled(act, ("V", t))
                free_bank(act.activation(V[:, t, :], ps[:, :], ACT.Copy), ("V", t))
            for t in range(T):
                for n in range(2):
                    ps = filled(act, ("q", t, n))
                    free_bank(act.activation(qs[:, t, 4 * n:4 * n + 4].rearrange("p h w -> p (h w)"), ps[:, 0:384],
                                             ACT.Copy, scale=float(QD) ** -0.5), ("q", t, n))
            for i in (0, 2):
                ps = filled(act, ("AB", i))
                free_bank(act.activation(AB[:, i // 2, i % 2], ps[:, :], ACT.Copy), ("AB", i))
            ps = filled(act, "M")
            free_bank(act.activation(fM.rearrange("p a b n -> p (a b n)"), ps[:, :], ACT.Copy), "M")
            for t in range(T):
                ps = filled(act, ("fy", t))
                free_bank(act.activation(MIX[:, t, 256:512], ps[:, 0:256], ACT.Copy), ("fy", t))
            for h in range(GH):
                ps = filled(act, ("o", h))
                act.activation(osq[:, h], ps[:, 0:T * GDV].rearrange("p (t v) -> p t v", t=T), ACT.Square).then_inc(squares_ready, 1)
            root_guess(rgla[:, 1], rgla[:, 0])
            for h in range(0, MH, 2):
                ps = filled(act, ("qT", h))
                free_bank(act.activation(qT[0:QD, h, :], ps[0:QD, :], ACT.Copy), ("qT", h))
            for i in range(T * MH):
                ps = filled(act, ("S", i))
                act.wait_ge(neg_max, i + 1)
                if i >= 2:
                    act.wait_ge(bank_full[PLAN[("PT", i - 2)][0]], PLAN[("PT", i - 2)][1])
                free_bank(act.activation(probs[:, i % 2], ps[:, :], ACT.Exp, bias=nm[:, i:i + 1],
                                         accum_out=rs[:, i:i + 1]), ("S", i))
            for c in range(0, C, 2):
                ps = filled(act, ("mT", c))
                free_bank(act.activation(xnT[:, c, :], ps[:, :], ACT.Copy), ("mT", c))
            for step in OUT_ORDER:
                kind, t = step[0:2]
                if kind == "out":
                    n = step[2]
                    drained(act, step)
                    act.activation(sqj[:, n * 512:(n + 1) * 512], X[:, t, n * 512:(n + 1) * 512], ACT.Square,
                                   scale=float(D) ** -0.5, accum_out=rn2[:, t, 4 * n:4 * n + 1]).then_inc(squares_ready, 1)
                    act.wait_ge(squares_ready, SQ2 + 2 * t + n + 1)
                    if n == 1:
                        root_guess(rn2[:, t, 2:3], rn2[:, t, 1:2])
                elif kind == "T":
                    for q in range(1 if t == T - 1 else 2):
                        ps = filled(act, ("x2T", t, q))
                        free_bank(act.activation(xnT[:, 4 * q:4 * q + 4, t * P:(t + 1) * P],
                                                 ps[:, :].rearrange("p (c n) -> p c n", c=4), ACT.Copy), ("x2T", t, q))
                elif kind == "Lf":
                    ps = filled(act, step)
                    if t >= 2:
                        act.wait_ge(bank_full[PLAN[("L", t - 2)][0]], PLAN[("L", t - 2)][1])
                    free_bank(act.activation(lf[:, t % 2], ps[:, 0:P], ACT.Copy), step)
                elif kind == "pos":
                    act.wait_ge(logit_ready, 2 * t + 1)
                    act.activation(rt[:, t, 1, 0:NG], lg[:, t, 0:NG], ACT.Exp, bias=rt[:, t, 0, 3:4],
                                   accum_out=rt[:, t, 0, 0:1]).then_inc(rexp_ready, 1)
                    act.wait_ge(logit_ready, 2 * t + 2)
                    act.activation(rt[:, t, 0, 4:5], rt[:, t, 0, 5:6], ACT.Exp).then_inc(rexp_ready, 1)
            act.preload_act_table_set("silu_and_others")

            def expert(e, slot):
                act.wait_ge(gu_full, e + 1)
                if not (isinstance(e, int) and e < 2):
                    act.wait_ge(hg_ready, e - 1)
                act.activation(hs[:, slot % 2], banks[2 + slot % 2][:, 0:P], ACT.Silu).then_inc(silu_done, 1)

            def copy_gathered(buf, par):
                return act.activation(xeT[:, buf, :, par * BLOCK:(par + 1) * BLOCK].rearrange("p (h j) s -> p h j s", h=2),
                                      banks[par][:, :].rearrange("p (j h s) -> p h j s", j=4, h=2), ACT.Copy)

            def copy_tokens(k, half, buf, pick):
                act.wait_ge(xe_full, k + 1)
                if pick:
                    ins = act.activation(xeT[:, buf, 4 * half:4 * half + 4],
                                         banks[half][:, :].rearrange("p (j s) -> p j s", j=4), ACT.Copy)
                else:
                    ins = copy_gathered(buf, half)
                ins.then_inc(xe_ready, 1)

            for half in range(2):
                copy_tokens(half, half, 0, True)

            def step(e, s, pick):
                expert(e, s)
                if not (isinstance(e, int) and e >= NE - 2):
                    copy_tokens(e + 2, s % 2, 1 - s // 2, pick)

            for e in range(2 * RING):
                step(e, e % RING, picked(e // 2 + 1))
            with act.Fori(2, NE // RING - 1) as i:
                for s in range(RING):
                    step(i * RING + s, s, True)
            for e in range(NE - RING, NE):
                step(e, e % RING, picked(e // 2 + 1))
            act.wait_ge(nmax_ready, 1)
            act.wait_ge(y_ready, NE)
            with act.If(act.value_load(nmax[0:1, 0:1]) > BLOCK):
                with act.Fori(0, NE * OVB) as n:
                    act.wait_ge(ov_xt, n + 1)
                    copy_gathered(0, 0).then_inc(ov_xc, 1)
                    act.wait_ge(ov_gu, n + 1)
                    act.activation(hs[:, 0], banks[2][:, 0:P], ACT.Silu).then_inc(ov_silu, 1)
            act.preload_act_table_set("natural_log_exp_and_others")
            def finish(t):
                act.wait_ge(root_ready, t + 1)
                act.wait_ge(x3_gain, t + 1)
                act.activation(X[:, t, :], MIX[:, t, :], ACT.Copy, scale=stat[:, 56 + t:57 + t]).then_inc(out_ready, 1)

            for t in range(T):
                act.wait_ge(x3_ready, t + 1)
                act.activation(sqj, X[:, t, :], ACT.Square, accum_out=stat[:, 48 + t:49 + t]).then_inc(squares_ready, 1)
                act.wait_ge(squares_ready, SQ3 + t + 1)
                root_guess(stat[:, 56 + t:57 + t], stat[:, 52 + t:53 + t])
                if 1 <= t < T - 1:
                    finish(t - 1)
            finish(T - 2)
            finish(T - 1)

        @block.vector
        def _(dve):
            link = linker(dve, dve_chain)
            norms = [0]

            def variance(dst, ss, n):
                dve.tensor_scalar(dst, ss, 1.0 / n, EPS, ALU.mult, ALU.add).then_inc(var_ready, 1)
                norms[0] += 1

            def refine(guess, var, tmp):
                dve.wait_ge(guess_ready, norms[0])
                link(dve.tensor_tensor(tmp, guess, guess, ALU.mult))
                link(dve.scalar_tensor_tensor(tmp, tmp, -0.5, var, ALU.mult, ALU.mult))
                link(dve.scalar_tensor_tensor(guess, tmp, 1.5, guess, ALU.add, ALU.mult))

            dve.wait_ge(first_landed, 64)
            ang = ropet[:, 0]
            kk = ropet[:, 1]
            link(dve.tensor_copy(posf[:, :], posi[:, :]))
            link(dve.tensor_tensor(ang, posf[:, :].unsqueeze(2).to_broadcast([P, T, HALF]),
                                   small[:, 49:65].unsqueeze(1).to_broadcast([P, T, HALF]), ALU.mult))
            link(dve.tensor_scalar(kk, ang, float(1.0 / (2.0 * np.pi)), MAGIC, ALU.mult, ALU.add))
            link(dve.tensor_scalar(kk, kk, MAGIC, None, ALU.subtract))
            for part in TWO_PI_PARTS:
                link(dve.scalar_tensor_tensor(ang, kk, -part, ang, ALU.mult, ALU.add))
            link(dve.tensor_scalar(ang, ang, 3.1415925, -3.1415925, ALU.min, ALU.max))
            link(dve.scalar_tensor_tensor(kk, ang, -1.0, ang, ALU.mult, ALU.min))
            dve.tensor_scalar(kk, kk, float(np.pi / 2), None, ALU.add).then_inc(angles_ready, 1)

            dve.wait_ge(squares_ready, T)
            variance(stat[:, 4:8], stat[:, 0:4], D)
            dve.wait_ge(var_ready, 1)
            refine(stat[:, 8:12], stat[:, 4:8], stat[:, 12:16])
            for t in range(T):
                dve.wait_ge(x_landed[t], 16)
                dve.tensor_scalar(MIX[:, t, :], X[:, t, :], stat[:, 8 + t:9 + t], None, ALU.mult).then_inc(xn_ready, 1)
            for c in range(1, C, 2):
                ps = filled(dve, ("xT", c))
                free_bank(dve.tensor_scalar(xnT[:, c, :], ps[:, :], gain1[:, c:c + 1], None, ALU.mult), ("xT", c))
            ps = filled(dve, ("pT", 1))
            free_bank(dve.tensor_scalar(qg, ps[:, :], float(GDK) ** -0.5, None, ALU.mult), ("pT", 1))
            ps = filled(dve, ("pT", 2))
            free_bank(dve.tensor_copy(kg, ps[:, :]), ("pT", 2))

            def copy_ucq(t):
                ps = filled(dve, ("ucq", t))
                free_bank(dve.tensor_copy(ucq[:, t, :], ps[:, :]), ("ucq", t))

            copy_ucq(0)
            dve.wait_ge(consts_landed, 16 * N_CONSTS)
            for dd in range(2):
                ps = filled(dve, ("z", dd))
                free_bank(dve.tensor_scalar(la[:, dd], ps[:, :], ba[:, dd:dd + 1], None, ALU.add), ("z", dd))
                drained(dve, ("z", dd))
                dve.scalar_tensor_tensor(gexp[:, dd, 0], la[:, dd], -1.0, la[:, dd], ALU.mult, ALU.min).then_inc(gate_abs, 1)
            dve.wait_ge(keep_ready, 1)
            for dd in range(2):
                dve.wait_ge(gate_log, dd + 1)
                link(dve.scalar_tensor_tensor(la[:, dd], la[:, dd], 0.0, gexp[:, dd, 1], ALU.min, ALU.subtract))
                link(dve.tensor_tensor_scan(cum[:, dd], keep, la[:, dd], 0.0, ALU.mult, ALU.add))
                ends = cum[:, dd].rearrange("p (n s) -> p n s", s=CHUNK)[:, :, CHUNK - 1]
                if dd == 0:
                    dve.tensor_copy(tot[:, dd], ends).then_inc(decay_sum, 1)
                else:
                    link(dve.tensor_copy(tot[:, dd], ends))
                    link(dve.tensor_tensor(la[:, dd], la[:, dd], cum[:, dd], ALU.subtract))
                    dve.tensor_tensor(cum[:, dd].rearrange("p (n s) -> p n s", s=CHUNK),
                                      la[:, dd].rearrange("p (n s) -> p n s", s=CHUNK),
                                      tot[:, dd].unsqueeze(2).to_broadcast([P, NCH, CHUNK]), ALU.add).then_inc(decay_sum, 1)
            copy_ucq(1)
            for dd in range(2):
                dve.wait_ge(decay_exp, 3 * dd + 3)
                if dd == 0:
                    drained(dve, ("pT", 1))
                    drained(dve, ("pT", 2))
                dve.tensor_tensor(qdec[:, dd], qg, gexp[:, dd, 0], ALU.mult).then_inc(gla_ready, 1)
                dve.tensor_tensor(kinv[:, dd], kg, gexp[:, dd, 1], ALU.mult).then_inc(gla_ready, 1)
                dve.wait_ge(gla_ready, 3 * dd + 2)
                dve.tensor_tensor(gexp[:, dd, 0].rearrange("p (n s) -> p n s", s=CHUNK),
                                  kinv[:, dd].rearrange("p (n s) -> p n s", s=CHUNK),
                                  dec[:, dd].unsqueeze(2).to_broadcast([P, NCH, CHUNK]), ALU.mult).then_inc(gla_ready, 1)
            copy_ucq(2)
            copy_ucq(3)
            dve.wait_ge(squares_ready, T + 8)
            link(dve.tensor_scalar(stat[:, 24:28], stat[:, 16:20], 1.0 / 256, EPS, ALU.mult, ALU.add))
            variance(stat[:, 28:32], stat[:, 20:24], 128)
            dve.wait_ge(var_ready, norms[0])
            refine(stat[:, 32:40], stat[:, 24:32], stat[:, 40:48])
            for t in range(T):
                drained(dve, ("ucq", t))
                dve.tensor_scalar(ucq[:, t, 256:512], ucq[:, t, 256:512], stat[:, 32 + t:33 + t], None,
                                  ALU.mult).then_inc(latents_ready, 1)
                dve.tensor_scalar(ckr[:, t, 0:128], ckr[:, t, 0:128], stat[:, 36 + t:37 + t], None,
                                  ALU.mult).then_inc(latents_ready, 1)
            gg = vg[:, :, 256:512]
            dve.wait_ge(silu_exp, 1)
            link(dve.tensor_scalar(sgt, sgt, 1.0, None, ALU.add))
            link(dve.reciprocal(sgt, sgt))
            link(dve.tensor_tensor(gg, gg, sgt, ALU.mult))
            for t in range(T):
                gt = vg[:, t, 256:512].rearrange("p (h v) -> p h v", h=GH)
                link(dve.tensor_tensor(gt, gt, gain_gla[:, :].unsqueeze(1).to_broadcast([P, GH, GDV]), ALU.mult))
            for c in range(2):
                ps = filled(dve, ("cqT", c))
                free_bank(dve.tensor_scalar(cqT[:, c, :], ps[:, :], gainq[:, c:c + 1], None, ALU.mult), ("cqT", c))
            for h in range(1, MH, 2):
                ps = filled(dve, ("kT", h))
                free_bank(dve.tensor_copy(kT[0:NOPE, h, :], ps[0:NOPE, :]), ("kT", h))
            for t in range(1, T, 2):
                ps = filled(dve, ("V", t))
                free_bank(dve.tensor_copy(V[:, t, :], ps[:, :]), ("V", t))
            for i in (1, 3):
                ps = filled(dve, ("AB", i))
                free_bank(dve.tensor_copy(AB[:, i // 2, i % 2], ps[:, :]), ("AB", i))
            for dd in range(2):
                ps = filled(dve, ("kendT", dd))
                free_bank(dve.tensor_copy(kend_tok[:, dd].rearrange("p t n -> p (t n)"), ps[:, :]), ("kendT", dd))
            for dd in range(2):
                ps = [filled(dve, ("kv", dd, odd)) for odd in range(2)]
                order = range(NCH - 1) if dd == 0 else range(NCH - 1, 0, -1)
                for i, n in enumerate(order):
                    to = n + 1 if dd == 0 else n - 1
                    kv = ps[n % 2][:, n // 2 * GDV:(n // 2 + 1) * GDV]
                    if i == 0:
                        ins = dve.tensor_copy(state[:, dd, to, :], kv)
                    else:
                        ins = dve.scalar_tensor_tensor(state[:, dd, to, :], state[:, dd, n, :], dec[:, dd, n:n + 1], kv,
                                                       ALU.mult, ALU.add)
                    if i < NCH - 3:
                        link(ins)
                    else:
                        free_bank(ins, ("kv", dd, n % 2))
                        drained(dve, ("kv", dd, n % 2))
            dve.wait_ge(att_zero, 1)
            for tp in range(2):
                for h in range(GH):
                    ps = filled(dve, ("att", tp, h))
                    for dd in range(2):
                        ins = dve.copy_predicated(att[:, 2 * tp:2 * tp + 2, h, :],
                                                  mask[:, dd, :].unsqueeze(1).to_broadcast([P, 2, P]),
                                                  ps[:, dd * 2 * P:(dd + 1) * 2 * P].rearrange("p (t n) -> p t n", t=2))
                        if dd == 0:
                            link(ins)
                    free_bank(ins, ("att", tp, h))
            dve.wait_ge(squares_ready, T + 8 + GH)
            for h in range(GH):
                link(dve.tensor_reduce(rgla[:, 3, h * T:(h + 1) * T], osq[:, h], AX, ALU.add))
            variance(rgla[:, 0], rgla[:, 3], GDV)
            dve.wait_ge(var_ready, norms[0])
            refine(rgla[:, 1], rgla[:, 0], rgla[:, 2])
            for h in range(GH):
                ps = filled(dve, ("o", h))
                mx = MIX[:, :, h * GDV:(h + 1) * GDV]
                free_bank(dve.tensor_tensor(mx, ps[:, 0:T * GDV].rearrange("p (t v) -> p t v", t=T),
                                            rgla[:, 1, h * T:(h + 1) * T].unsqueeze(2).to_broadcast([P, T, GDV]),
                                            ALU.mult), ("o", h))
            for h in range(GH):
                drained(dve, ("o", h))
            dve.tensor_tensor(MIX[:, :, 0:256], MIX[:, :, 0:256], gg, ALU.mult).then_inc(gla_out, 1)
            for h in range(1, MH, 2):
                ps = filled(dve, ("qT", h))
                free_bank(dve.tensor_copy(qT[0:QD, h, :], ps[0:QD, :]), ("qT", h))
            for i in range(T * MH + 3):
                if i < T * MH:
                    ps = filled(dve, ("S", i))
                    dve.tensor_reduce(nm[:, i:i + 1], ps[:, :], AX, ALU.max, negate=True).then_inc(neg_max, 1)
                j = i - 2
                if 0 <= j < T * MH:
                    ps = filled(dve, ("PT", j))
                    if j >= 2:
                        dve.wait_ge(av_done, j - 1)
                    free_bank(dve.tensor_copy(probsT[:, j % 2], ps[:, :]), ("PT", j))
                j = i - 3
                if j >= 0 and j % MH == MH - 1:
                    tq = j // MH
                    ps = banks[PLAN[("O", tq)][0]]
                    dve.wait_ge(av_done, (tq + 1) * MH)
                    drained(dve, ("S", tq * MH + MH - 1))
                    link(dve.reciprocal(ri[:, tq * MH:(tq + 1) * MH], rs[:, tq * MH:(tq + 1) * MH]))
                    o = MIX[:, tq, 512:1024].rearrange("p (h v) -> p h v", h=MH)
                    free_bank(dve.tensor_tensor(o, ps[:, :].rearrange("p (h v) -> p h v", h=MH),
                                                ri[:, tq * MH:(tq + 1) * MH].unsqueeze(2).to_broadcast([P, MH, MV]),
                                                ALU.mult), ("O", tq))
            for c in range(1, C, 2):
                ps = filled(dve, ("mT", c))
                free_bank(dve.tensor_copy(xnT[:, c, :], ps[:, :]), ("mT", c))

            def first_max(vals, k, t, r, onehot, m):
                link(dve.tensor_reduce(m, vals, AX, ALU.max))
                a = rt[:, t, r, 0:k]
                b = rt[:, t, 0, 12:13]
                link(dve.scalar_tensor_tensor(a, vals, m, rank[:, 0:k], ALU.is_equal, ALU.mult))
                link(dve.tensor_reduce(b, a, AX, ALU.min))
                return dve.tensor_scalar(onehot, a, b, None, ALU.is_equal)

            def choose(first, buf):
                e = slice(first, first + 2) if isinstance(first, int) else bass.ds(first, 2)
                dve.tensor_tensor(sel[:, buf], pos1[:, :, e].unsqueeze(3).to_broadcast([P, T, 2, BLOCK]),
                                  small[:, ONE_UP:].unsqueeze(1).unsqueeze(1).to_broadcast([P, T, 2, BLOCK]),
                                  ALU.is_equal).then_inc(sel_ready, 1)

            for step in OUT_ORDER:
                kind, t = step[0:2]
                if kind == "out":
                    n = step[2]
                    ps = filled(dve, step)
                    xs = X[:, t, n * 512:(n + 1) * 512]
                    free_bank(dve.tensor_tensor(xs, ps[:, :], xs, ALU.add), step)
                    if n == 0:
                        continue
                    drained(dve, ("out", t, 0))
                    drained(dve, ("out", t, 1))
                    dve.wait_ge(squares_ready, SQ2 + 2 * t + 2)
                    dve.tensor_scalar(rn2[:, t, 1:2], rn2[:, t, 0:1], rn2[:, t, 4:5], EPS, ALU.add, ALU.add).then_inc(var_ready, 1)
                    norms[0] += 1
                    dve.wait_ge(var_ready, norms[0])
                    refine(rn2[:, t, 2:3], rn2[:, t, 1:2], rn2[:, t, 3:4])
                    if t == 0:
                        for c in range(C):
                            drained(dve, ("mT", c))
                        dve.wait_ge(g2_landed, 16)
                    dve.scalar_tensor_tensor(MIX[:, t, :].rearrange("p (c q) -> p q c", c=C),
                                             X[:, t, :].rearrange("p (q c) -> p q c", c=C), rn2[:, t, 2:3],
                                             g2b[:, :].rearrange("p (q c) -> p q c", c=C),
                                             ALU.mult, ALU.mult).then_inc(x2_ready, 1)
                elif kind == "T":
                    if t == T - 1:
                        ps = filled(dve, ("x2T", t, 1))
                        free_bank(dve.tensor_copy(xnT[:, 4:8, t * P:(t + 1) * P],
                                                  ps[:, :].rearrange("p (c n) -> p c n", c=4)), ("x2T", t, 1))
                elif kind == "L":
                    ps = filled(dve, step)
                    free_bank(dve.tensor_tensor(lg[:, t, :], ps[:, 0:NG + NE], rbias[:, :], ALU.add), step)
                    drained(dve, step)
                    sc = rt[:, t, 0]
                    ohg, l32 = rt[:, t, 2, 0:NG], rt[:, t, 4]
                    dve.tensor_reduce(sc[:, 3:4], lg[:, t, 0:NG], AX, ALU.max, negate=True).then_inc(logit_ready, 1)
                    link(first_max(lg[:, t, 0:NG], NG, t, 3, ohg, sc[:, 2:3]))
                    link(dve.tensor_scalar(ohg, ohg, -NBIG, NBIG, ALU.mult, ALU.add))
                    link(dve.tensor_tensor(l32.rearrange("p (g e) -> p g e", g=NG),
                                           lg[:, t, NG:].rearrange("p (g e) -> p g e", g=NG),
                                           ohg.unsqueeze(2).to_broadcast([P, NG, EPG]), ALU.add))
                    link(first_max(l32, NE, t, 8, oh[:, t, 0], sc[:, 6:7]))
                    link(dve.scalar_tensor_tensor(l32, oh[:, t, 0], 4 * NBIG, l32, ALU.mult, ALU.add))
                    link(first_max(l32, NE, t, 9, oh[:, t, 1], sc[:, 7:8]))
                    dve.tensor_tensor(mska[:, t], oh[:, t, 0], oh[:, t, 1], ALU.add).then_inc(picks_ready, 1)
                    dve.tensor_tensor(sc[:, 5:6], sc[:, 7:8], sc[:, 6:7], ALU.subtract).then_inc(logit_ready, 1)
                elif kind == "pos":
                    ps = filled(dve, step)
                    link(dve.scalar_tensor_tensor(pos1[:, t], ps[:, 0:NE], 1.0, mska[:, t], ALU.add, ALU.mult))
                    dve.tensor_tensor(sel0[:, t], pos1[:, t, 0:2].unsqueeze(2).to_broadcast([P, 2, BLOCK]),
                                      small[:, ONE_UP:].unsqueeze(1).to_broadcast([P, 2, BLOCK]),
                                      ALU.is_equal).then_inc(sel_ready, 1)
                    row, rows2 = rt[:, t, 10], rt[:, t, 11:13]
                    free_bank(dve.tensor_tensor(row, ps[:, 0:NE], small[:, 0:NE], ALU.add), step)
                    drained(dve, step)
                    link(dve.tensor_tensor(rows2, oh[:, t], row.unsqueeze(1).to_broadcast([P, 2, NE]), ALU.mult))
                    link(dve.tensor_reduce(rt[:, t, 0, 10:12], rows2, AX, ALU.add))
                    dve.tensor_copy(dest[:, t, :], rt[:, t, 0, 10:12]).then_inc(dest_ready, 1)
                    sc = rt[:, t, 0]
                    dve.wait_ge(rexp_ready, 2 * t + 2)
                    link(dve.tensor_scalar(sc[:, 8:9], sc[:, 4:5], 1.0, sc[:, 0:1], ALU.add, ALU.mult))
                    link(dve.reciprocal(wts[:, t, 0:1], sc[:, 8:9]))
                    link(dve.tensor_tensor(wts[:, t, 1:2], wts[:, t, 0:1], sc[:, 4:5], ALU.mult))
            ps = filled(dve, "count")
            free_bank(dve.tensor_reduce(lv[:, 0, 0:1], ps[:, 0:NE], AX, ALU.max), "count")
            drained(dve, "count")
            dve.tensor_copy(nmax[:, :], lv[:, 0, 0:1]).then_inc(nmax_ready, 1)

            choose(2, 1)
            ps = filled(dve, "listT")
            dve.wait_ge(nmax_ready, 1)
            free_bank(dve.tensor_copy(lv[:, 2], ps[:, 0:NE]), "listT")
            drained(dve, "listT")
            link(dve.tensor_scalar(lv[:, 0], lv[:, 2], float(S), -2.0 * S, ALU.is_ge, ALU.mult))
            link(dve.tensor_scalar(lv[:, 1], lv[:, 2], 2.0, small[:, 40:41], ALU.mult, ALU.add))
            link(dve.tensor_copy(sidx[:, :], lv[:, 1]))
            dve.tensor_tensor(gidx[:, :], lv[:, 1], lv[:, 0], ALU.add).then_inc(idx_ready, 1)

            def gated(e, slot):
                dve.wait_ge(silu_done, e + 1)
                if not (isinstance(e, int) and e < 2):
                    dve.wait_ge(hT_full, e - 1)
                dve.tensor_tensor(hg[:, slot % 2], hs[:, slot % 2], banks[2 + slot % 2][:, P:2 * P],
                                  ALU.mult).then_inc(hg_ready, 1)

            def copy_h(e, slot):
                dve.wait_ge(hT_full, e + 1)
                if not (isinstance(e, int) and e < 2):
                    dve.wait_ge(y_full, e - 1)
                dve.tensor_copy(hT[:, slot % 2].rearrange("p m s -> p (m s)"),
                                banks[6 + slot % 2][:, 0:P]).then_inc(hT_ready, 1)

            def copy_y(e, turn2, slot):
                dve.wait_ge(y_full, e + 1)
                if not (isinstance(e, int) and e < 2):
                    dve.wait_ge(y_stored[slot % 2], turn2 * 16)
                dve.tensor_copy(Y[:, slot % 2], banks[4 + slot % 2][:, :]).then_inc(y_ready, 1)

            def step(e, turn, s):
                known = isinstance(e, int)
                gated(e, s)
                if not (known and e < 1):
                    copy_y(e - 1, turn * (RING // 2) + (s - 1) // 2, (s - 1) % RING)
                copy_h(e, s)
                if s % 2 == 0 and not (known and (e + 4 >= NE or not picked(e // 2 + 2))):
                    dve.wait_ge(xe_full, e + 2)
                    choose(e + 4, s // 2)

            for e in range(2 * RING):
                step(e, e // RING, e % RING)
            with dve.Fori(2, NE // RING - 1) as i:
                for s in range(RING):
                    step(i * RING + s, i, s)
            for e in range(NE - RING, NE):
                step(e, NE // RING - 1, e % RING)
            copy_y(NE - 1, (NE - 1) // 2, RING - 1)
            dve.wait_ge(nmax_ready, 1)
            with dve.If(dve.value_load(nmax[0:1, 0:1]) > BLOCK):
                with dve.Fori(0, NE * OVB) as n:
                    dve.wait_ge(ov_list, n * 32 + 32)
                    dve.tensor_scalar(ovl[:, 1:2], ovl[:, 0:1], float(S), -2.0 * S, ALU.is_ge, ALU.mult).then_inc(ov_tmp, 1)
                    dve.tensor_scalar(ovl[:, 2:3], ovl[:, 0:1], 2.0, small[:, 40:41], ALU.mult, ALU.add).then_inc(ov_tmp, 1)
                    dve.wait_ge(ov_tmp, n * 2 + 2)
                    dve.tensor_copy(ov_s[:, :], ovl[:, 2:3]).then_inc(ov_idx, 1)
                    dve.tensor_tensor(ov_g[:, :], ovl[:, 2:3], ovl[:, 1:2], ALU.add).then_inc(ov_idx, 1)
                    dve.wait_ge(ov_silu, n + 1)
                    dve.tensor_tensor(hg[:, 0], hs[:, 0], banks[2][:, P:2 * P], ALU.mult).then_inc(ov_hg, 1)
                    dve.wait_ge(ov_hT, n + 1)
                    dve.tensor_copy(hT[:, 0].rearrange("p m s -> p (m s)"), banks[6][:, 0:P]).then_inc(ov_hc, 1)
                    dve.wait_ge(ov_y, n + 2)
                    dve.tensor_copy(Y[:, 0], banks[4][:, :]).then_inc(ov_yc, 1)

            def mean_square(t):
                dve.wait_ge(squares_ready, SQ3 + t + 1)
                variance(stat[:, 52 + t:53 + t], stat[:, 48 + t:49 + t], D)
                dve.wait_ge(var_ready, norms[0])

            def root(t):
                dve.wait_ge(guess_ready, norms[0])
                guess, tmp = stat[:, 56 + t:57 + t], stat[:, 60 + t:61 + t]
                link(dve.tensor_tensor(tmp, guess, guess, ALU.mult))
                link(dve.scalar_tensor_tensor(tmp, tmp, -0.5, stat[:, 52 + t:53 + t], ALU.mult, ALU.mult))
                dve.scalar_tensor_tensor(guess, tmp, 1.5, guess, ALU.add, ALU.mult).then_inc(root_ready, 1)

            for t in range(T):
                dve.wait_ge(pair_landed[t][0], 16)
                link(dve.scalar_tensor_tensor(X[:, t, :], ypair[:, t, 0], wts[:, t, 0:1], X[:, t, :], ALU.mult, ALU.add))
                if t >= 1:
                    mean_square(t - 1)
                dve.wait_ge(pair_landed[t][1], 16)
                dve.scalar_tensor_tensor(X[:, t, :], ypair[:, t, 1], wts[:, t, 1:2], X[:, t, :],
                                         ALU.mult, ALU.add).then_inc(x3_ready, 1)
                if t >= 1:
                    root(t - 1)
            mean_square(T - 1)
            root(T - 1)

        @block.gpsimd
        def _(pool):
            link = linker(pool, pool_chain)

            def hold():
                pool.tensor_tensor(held[:, 0:1], held[:, 1:2], held[:, 1:2], ALU.add).then_inc(held_done, 1)

            pool.memset(held[:, :], 0.0).then_inc(held_done, 1)
            pool.memset(wa[:, :, :], 0.0).then_inc(gatew_zero, 1)
            pool.memset(wr[:, :, :], 0.0).then_inc(gatew_zero, 1)
            link(pool.memset(keep, 1.0))
            pool.memset(keep.rearrange("p (n s) -> p n s", s=CHUNK)[:, :, 0:1], 0.0).then_inc(keep_ready, 1)
            link(pool.memset(krp[:, :, 0:NOPE], 0.0))
            pool.memset(lfill[:, :], EMPTY).then_inc(fill_ready, 1)
            for t in range(T):
                drained(pool, ("vg", t))
            pool.memset(fw, 0.0).then_inc(fnetw_zero, 1)
            pool.memset(att.rearrange("p t h n -> p (t h n)"), 0.0).then_inc(att_zero, 1)

            def rotate(x1, x2, o1, o2, sin, cos, t1, t2, t3, t4):
                link(pool.tensor_tensor(t1, x1, cos, ALU.mult))
                link(pool.tensor_tensor(t2, x2, sin, ALU.mult))
                link(pool.tensor_tensor(t3, x1, sin, ALU.mult))
                link(pool.tensor_tensor(t4, x2, cos, ALU.mult))
                link(pool.tensor_tensor(o1, t1, t2, ALU.subtract))
                return pool.tensor_tensor(o2, t3, t4, ALU.add)

            pool.wait_ge(tables_ready, 2)
            for t in range(T):
                drained(pool, ("ckr", t))
            k1, k2 = ckr[:, :, 128:144], ckr[:, :, 144:160]
            tm = [rtmp[:, i].rearrange("p h w -> p (h w)")[:, 0:T * HALF].rearrange("p (t w) -> p t w", t=T) for i in range(4)]
            rotate(k1, k2, krp[:, :, NOPE:NOPE + HALF], krp[:, :, NOPE + HALF:], ropet[:, 0], ropet[:, 1],
                   *tm).then_inc(kr_rot, 1)
            pool.wait_ge(kr_rot, 1)
            for t in range(T):
                drained(pool, ("q", t, 0))
                drained(pool, ("q", t, 1))
                q1, q2 = qs[:, t, :, NOPE:NOPE + HALF], qs[:, t, :, NOPE + HALF:]
                sin = ropet[:, 0, t, :].unsqueeze(1).to_broadcast([P, MH, HALF])
                cos = ropet[:, 1, t, :].unsqueeze(1).to_broadcast([P, MH, HALF])
                rotate(q1, q2, q1, q2, sin, cos, *[rtmp[:, i] for i in range(4)]).then_inc(q_rot, 1)
                pool.wait_ge(q_rot, t + 1)
            pool.wait_ge(list_filled, 16)
            for t in range(T):
                pool.wait_ge(dest_ready, t + 1)
                for r in range(2):
                    pool.indirect_dma_start(list_d, bass.IndirectOffsetOnAxis(ap=dest[:, t, r:r + 1], axis=0),
                                            small[:, 41 + 2 * t + r:42 + 2 * t + r], None,
                                            bounds_check=NE * S - 1, oob_is_err=False).then_inc(scattered, 16)
            pool.wait_ge(idx_ready, 1)

            def scatter(e):
                pool.wait_ge(y_ready, e + 1)
                pool.indirect_dma_start(y_rows, bass.IndirectOffsetOnAxis(ap=sidx[:, e:e + 1], axis=0),
                                        Y[:, e % 2], None,
                                        bounds_check=4 * S - 1, oob_is_err=False).then_inc(y_stored[e % 2], 16)

            def gather(e):
                if e >= 2 * GATHERED[0] + 2:
                    pool.wait_ge(xe_full, e - 1)
                pool.indirect_dma_start(xg[e % 2], None, x2_rows,
                                        bass.IndirectOffsetOnAxis(ap=gidx[:, e:e + 1], axis=0),
                                        bounds_check=2 * S - 1, oob_is_err=False).then_inc(xg_landed[e % 2], 16)

            pool.wait_ge(x2_stored, 16 * T)
            gathers = list(range(2 * GATHERED[0], 2 * GATHERED[-1] + 2))
            for e in gathers[:2]:
                gather(e)
            for e in range(NE):
                scatter(e)
                if e + 2 < len(gathers):
                    gather(gathers[e + 2])
            for q in range(2):
                pool.wait_ge(y_stored[q], 16 * NE // 2)
            pool.wait_ge(nmax_ready, 1)
            with pool.If(pool.value_load(nmax[0:1, 0:1]) > BLOCK):
                with pool.Fori(0, NE * OVB) as n:
                    pool.wait_ge(held_done, n * 3 + 1)
                    pool.wait_ge(ov_idx, n * 2 + 2)
                    hold()
                    pool.indirect_dma_start(xg[0], None, x2_rows,
                                            bass.IndirectOffsetOnAxis(ap=ov_g[:, 0:1], axis=0),
                                            bounds_check=2 * S - 1, oob_is_err=False).then_inc(ov_x, 16)
                    pool.wait_ge(held_done, n * 3 + 2)
                    pool.wait_ge(ov_yc, n + 1)
                    hold()
                    pool.indirect_dma_start(y_rows, bass.IndirectOffsetOnAxis(ap=ov_s[:, 0:1], axis=0),
                                            Y[:, 0], None,
                                            bounds_check=4 * S - 1, oob_is_err=False).then_inc(ov_stored, 16)
                    pool.wait_ge(held_done, n * 3 + 3)
                    pool.wait_ge(ov_stored, n * 16 + 16)
                    hold()
                pool.wait_ge(held_done, NE * OVB * 3 + 1)
            pool.nop().then_inc(moe_done, 1)
            pool.wait_ge(gf_landed, 16)
            for t in range(T):
                pool.wait_ge(x3_ready, t + 1)
                pool.tensor_tensor(MIX[:, t, :], X[:, t, :], gfb, ALU.mult).then_inc(x3_gain, 1)


_INS = ["x", "positions", "norm1_g", "w_in", "gla_wa_f", "gla_ba_f", "gla_wa_b", "gla_ba_b", "gla_norm_g", "fnet_w",
        "mla_q_norm_g", "mla_w_uq", "mla_kv_norm_g", "mla_w_ukv", "w_out", "norm2_g", "moe_w_rg", "moe_b_rg",
        "moe_w_re", "moe_b_re", "moe_w_gate", "moe_w_up", "moe_w_down", "final_norm_g"]


def kernel(**inputs):
    import numpy as _np
    import concourse.bacc as _bacc
    from concourse import mybir as _mybir
    from concourse.bass_utils import run_bass_kernel_spmd as _run

    nc = _bacc.Bacc("TRN2", target_bir_lowering=False, num_devices=1)
    given = {name: _np.ascontiguousarray(inputs[name]) for name in _INS}
    given.update(shape_constants())
    arrays, aps = {}, {}
    for name, a in given.items():
        arrays[f"in_{name}"] = a
        aps[name] = nc.dram_tensor(f"in_{name}", a.shape, _mybir.dt.from_np(a.dtype), kind="ExternalInput").ap()
    out = nc.dram_tensor("out_0", (1, S, D), F32, kind="ExternalOutput").ap()
    encoder_kernel(nc, aps, out)
    return _run(nc, [arrays], core_ids=[0]).results[0]["out_0"]
```

```python
from contextlib import ExitStack

import numpy as np
import concourse.bass as bass
from concourse import mybir

F32 = mybir.dt.float32
I32 = mybir.dt.int32
ALU = mybir.AluOpType
ACT = mybir.ActivationFunctionType
AX = mybir.AxisListType.X

P = 128
D = 1024
S = 512
T = S // P
C = D // P
EPS = 1e-6
GQ, GK, GV, GG, GA, FU, CQ, CKV, KR, W_IN = 0, 128, 256, 512, 768, 800, 1056, 1312, 1440, 1472
GH, GDK, GDV, TAU, CHUNK = 4, 32, 64, 16.0, 64
NCH = S // CHUNK
FREQ = S // 2 + 1
MH, NOPE, ROPE, MV = 8, 64, 32, 64
QD = NOPE + ROPE
HALF = ROPE // 2
NG, EPG, NE, DE = 4, 8, 32, 256
BLOCK = 64
RING = 4
FIRST = RING + 2
TURNS = (NE - FIRST) // RING
GATHERED = (2, 3, 4)
OVB = S // BLOCK
STACK, ONE_UP, SMALL = 65, 65 + NG + NE, 65 + NG + NE + BLOCK
EMPTY = 4096.0
NBIG = -1.0e30
MAGIC = 12582912.0
TWO_PI_PARTS = (6.28125, 0.0019350051879882812, 3.019916e-07, -1.9551e-11)


def psum_plan():
    plan, fills, frees = {}, [0] * 8, [0] * 8

    def use(key, bank, readers=1, fill=1):
        fills[bank] += fill
        before = frees[bank]
        frees[bank] += readers
        plan[key] = (bank, fills[bank], before, frees[bank])

    turn = [0]

    def ring(key, readers=1):
        use(key, turn[0] % 8, readers)
        turn[0] += 1

    for c in range(C):
        ring(("xT", c))
    for i in (1, 2, 0):
        ring(("pT", i))
    for t in range(T):
        ring(("ckr", t))
        ring(("ucq", t))
        if t == 0:
            ring(("z", 0))
            ring(("z", 1))
    for t in range(T):
        ring(("vg", t))
    ring("ckvT")
    for c in range(2):
        ring(("cqT", c))
    for h in range(0, MH, 2):
        ring(("kT", h), readers=2)
    for t in range(T):
        ring(("V", t))
    ring("krT")
    for t in range(T):
        for n in range(2):
            ring(("q", t, n))
    for i in range(4):
        ring(("AB", i))
    ring("M")
    for t in range(T):
        ring(("fy", t))
    for d in range(2):
        ring(("kendT", d))
    for d in range(2):
        ring(("kv", d, 0))
        ring(("kv", d, 1))
    for t in range(T):
        for d in range(2):
            ring(("att", t, d))
    for h in range(MH):
        ring(("qT", h))
    for t in range(T):
        ring(("o", t))
    for kind, i in attention_order():
        if kind == "S":
            use(("S", i), i % 3)
        elif kind == "mT":
            use(("mT", i), (3, 4, 5, 7)[i])
        elif kind == "PT":
            use(("PT", i), 3 + i % 3)
        elif i % 4 == 0:
            use(("O", i // 4), 6 + i // 4 % 2, fill=0)
    turn[0] = 0

    def late(key):
        use(key, 2 + turn[0] % 6)
        turn[0] += 1

    for step in OUT_ORDER:
        if step[0] == "T":
            late(("x2T", step[1], 0))
            late(("x2T", step[1], 1))
        elif step[0] != "pick":
            late(step)
    late("count")
    late("listT")
    return plan, fills, frees


OUT_ORDER = [("out", 0, 0), ("out", 0, 1), ("out", 1, 0), ("T", 0), ("out", 1, 1), ("Lf", 0), ("out", 2, 0),
             ("L", 0), ("T", 1), ("out", 2, 1), ("pos", 0), ("Lf", 1), ("out", 3, 0), ("L", 1), ("T", 2),
             ("Lf", 2), ("L", 2), ("out", 3, 1), ("pick", 0), ("pos", 1), ("T", 3), ("pos", 2), ("Lf", 3), ("L", 3),
             ("pick", 1), ("pick", 2), ("pos", 3), ("pick", 3)]


def attention_order():
    steps = []
    for i in range(T * MH + 5):
        if i < T * MH:
            steps.append(("S", i))
        if i == 2:
            steps += [("mT", c) for c in range(4)]
        if i >= 6 and i % 2 == 0:
            steps.append(("AV", (i - 6) // 2))
        if 0 <= i - 3 < T * MH:
            steps.append(("PT", i - 3))
    return steps


def picked(pair):
    return pair not in GATHERED


def picks(pair):
    return sum(picked(q) for q in range(pair + 1))


def shape_constants():
    k = np.arange(S)
    ang = 2.0 * np.pi * ((k[:, None] * k[None, :]) % S) / S
    dft = np.stack([np.cos(ang), np.sin(ang)])[:, :, 0:FREQ] / np.sqrt(S)
    k = np.arange(64)
    ang = 2.0 * np.pi * ((k[:, None] * k[None, :]) % 64) / 64
    chan = np.zeros((P, 2, P))
    for g in range(2):
        chan[g * 64:g * 64 + 64, 0, g * 64:g * 64 + 64] = np.cos(ang) / 8.0
        chan[g * 64:g * 64 + 64, 1, g * 64:g * 64 + 64] = -np.sin(ang) / 8.0
    j, i = np.arange(P)[:, None], np.arange(P)[None, :]
    same = j // CHUNK == i // CHUNK
    mask = np.stack([same & (j <= i), same & (j > i)], axis=1)
    tri = np.stack([j < i, np.ones((P, P), bool)], axis=1)
    small = np.zeros((P, SMALL))
    small[:, ONE_UP:] = np.arange(BLOCK) + 1
    small[:, 0:32] = np.arange(NE) * S
    small[:, STACK:ONE_UP] = np.arange(P)[:, None] % 64 == np.arange(NG + NE)[None, :]
    small[:, 40] = np.arange(P) // BLOCK
    for t in range(T):
        for r in range(2):
            small[:, 41 + 2 * t + r] = r * S + t * P + np.arange(P)
    inv = (1.0 / (np.float32(10000.0) ** (np.arange(0, ROPE, 2, dtype=np.float32) / np.float32(ROPE))))
    small[:, 49:65] = inv.astype(np.float32)
    f = np.float32
    rank = np.tile(np.arange(NE) - 100.0, (P, 1))
    return {"c_rank": rank.astype(f), "c_ident": np.eye(P, dtype=f), "c_dft": dft.astype(f), "c_chan": chan.astype(f),
            "c_mask": mask.astype(np.int32), "c_tri": tri.astype(f), "c_small": small.astype(f)}


def encoder_kernel(nc, d, out):
    ctx = ExitStack()
    with ctx:
        def sb(name, shape, dt=F32):
            return ctx.enter_context(nc.sbuf_tensor(name, shape, dt))

        def sem(name):
            return ctx.enter_context(nc.semaphore(name))

        PLAN, FILLS, FREES = psum_plan()

        x_v = d["x"].rearrange("b (t p) n -> p (b t) n", p=P)
        out_v = out.rearrange("b (t p) n -> p (b t) n", p=P)
        w_in_v = d["w_in"][0].rearrange("(p c) n -> p c n", c=C)
        w_out_v = d["w_out"][0].rearrange("(c p) n -> p c n", c=C)
        w_gate_v = d["moe_w_gate"][0].rearrange("e (p c) n -> e p (c n)", c=C)
        w_up_v = d["moe_w_up"][0].rearrange("e (p c) n -> e p (c n)", c=C)
        w_down_v = d["moe_w_down"][0].rearrange("e (c p) n -> e p c n", c=2)
        x2_d = nc.dram_tensor("x2_scratch", (S, D), F32, kind="Internal").ap()
        list_d = nc.dram_tensor("list_scratch", (NE * S, 1), F32, kind="Internal").ap()
        y_d = nc.dram_tensor("y_scratch", (2 * S, D), F32, kind="Internal").ap()
        x2_rows = x2_d.rearrange("t (h n) -> (t h) n", h=2)
        y_rows = y_d.rearrange("t (h n) -> (t h) n", h=2)

        X = sb("X", [P, T, D])
        MIX = sb("MIX", [P, T, D])
        XT = sb("XT", [P, C * S])
        WO = sb("WO", [P, C * D])
        EW = sb("EW", [P, RING, 3, C * DE])
        G = sb("G", [P, 5632])
        ident = sb("ident", [P, P])
        mask = sb("mask", [P, 2, P], I32)
        tri = sb("tri", [P, 2, P])
        small = sb("small", [P, SMALL])
        pos1 = sb("pos1", [P, T, NE])
        rank = sb("rank", [P, NE])
        wr = sb("wr", [P, C, 64])
        rbias = sb("rbias", [P, NG + NE])
        gain1 = sb("gain1", [P, C])
        gainq = sb("gainq", [P, 2])
        gainkv = sb("gainkv", [P, 1])
        gain_gla = sb("gain_gla", [P, GDV])
        ba = sb("ba", [P, 2])
        stat = sb("stat", [P, 64])
        ropet = sb("ropet", [P, 2, T, HALF])
        wts = sb("wts", [P, T, 2])
        gidx = sb("gidx", [P, NE], I32)
        sidx = sb("sidx", [P, NE], I32)
        dest = sb("dest", [P, T, 2], I32)
        nmax = sb("nmax", [P, 1], I32)

        def view(region, start, shape):
            n = 1
            for s in shape:
                n *= s
            ap = region[:, start:start + n]
            if len(shape) == 1:
                return ap
            names = "abcd"[:len(shape)]
            return ap.rearrange(f"p ({' '.join(names)}) -> p {' '.join(names)}",
                                **{k: s for k, s in zip(names[1:], shape[1:])})

        xnT = view(XT, 0, (C, S))
        att = view(XT, 0, (T, GH, P))
        kend_tok = view(XT, 2048, (2, T, P))
        state = view(XT, 3072, (2, NCH, GDV))
        wof = WO[:, :]
        dft = view(WO, 0, (2, T, FREQ))
        AB = view(WO, 4096, (2, 2, S))
        gexp = view(WO, 6144, (2, 2, S))
        q_diag = view(WO, 0, (2, T, GH, P))
        state_diag = view(WO, 4096, (2, NCH, GH, GDV))
        osq = view(XT, 2048, (T, GH * GDV))
        w_out_sb = view(WO, 0, (C, D))
        ew01 = EW[:, 0:2].rearrange("p r w n -> p (r w n)")
        ew23 = EW[:, 2:4].rearrange("p r w n -> p (r w n)")
        w_in_sb = view(ew01, 0, (C, W_IN))
        qT = view(ew01, 0, (MH, S))
        kT = view(ew01, 4096, (MH, S))
        V = view(ew01, 8192, (T, MH * MV))
        fw = view(ew01, 10240, (2, P))
        chan = view(ew01, 10496, (2, P))
        fM = view(ew01, 10752, (2, 2, P))
        rtmp = view(ew01, 11264, (4, MH, HALF))
        ucq = view(ew23, 0, (T, 512))
        vg = view(ew23, 2048, (T, 512))
        ckr = view(ew23, 4096, (T, 160))
        krp = view(ew23, 4736, (T, QD))
        w_uq = view(ew23, 5120, (2, MH * QD))
        w_ukv = view(ew23, 6656, (MH, NOPE + MV))
        cqT = view(ew23, 7680, (2, S))
        ckvT = view(ew23, 8704, (S,))
        qs = view(ew23, 9216, (T, MH, QD))
        qg = view(G, 0, (S,))
        kg = view(G, 512, (S,))
        la = view(G, 1024, (2, S))
        cum = view(G, 2048, (2, S))
        qdec = view(G, 3072, (2, S))
        kinv = view(G, 4096, (2, S))
        probs = view(G, 0, (4, S))
        probsT = view(G, 2048, (4, S))
        keep = view(G, 5120, (S,))
        gaT = ew23[:, 9600:10112]
        wa = ew23[:, 10112:10368].rearrange("p (a n) -> p a n", a=2)
        squares_out = view(ew23, 9216, (256,))
        sgt = view(ew01, 0, (T, 256))
        posi = sb("posi", [P, T], I32)
        posf = sb("posf", [P, T])
        rgla = sb("rgla", [P, 4, GH * T])
        nm = sb("nm", [P, T * MH])
        rs = sb("rs", [P, T * MH])
        ri = sb("ri", [P, T * MH])
        lfill = sb("lfill", [P, P])
        held = sb("held", [P, 2])
        g2b = view(G, 4608, (D,))
        sqj = view(G, 3584, (D,))
        tot = sb("tot", [P, 2, NCH])
        dec = sb("dec", [P, 2, NCH])
        xeT = view(WO, 6144, (2, C, P))
        sel = view(G, 4608, (2, T, 2, BLOCK))
        sel0 = view(G, 2560, (T, 2, BLOCK))
        Y = view(G, 2560, (2, 512))
        hs = view(G, 3584, (2, P))
        hg = view(G, 3840, (2, P))
        hT = view(G, 4096, (2, 2, BLOCK))
        gfb = view(XT, 0, (D,))
        xg = [G[:, 2048:2560], G[:, 4608:5120]]
        gu_at = [EW[:, s, 0:2].rearrange("p w n -> p (w n)") for s in range(RING)]
        gu_at += [WO[:, 0:2 * C * DE], XT[:, 0:2 * C * DE]]
        dn_at = [EW[:, s, 2] for s in range(RING)] + [WO[:, 2 * C * DE:3 * C * DE], G[:, 0:C * DE]]
        lg = view(G, 0, (T, NG + NE))
        rt = view(G, 160, (T, 14, NE))
        mska = view(G, 2048, (T, NE))
        oh = view(G, 2176, (T, 2, NE))
        lst = G[0:NE, 2432:2560]
        rn2 = view(G, 3080, (T, 8))
        lv = view(G, 4352, (3, NE))
        lf = view(G, 3120, (2, P))
        ovl = view(G, 4448, (4,))
        ov_g = sb("ov_g", [P, 1], I32)
        ov_s = sb("ov_s", [P, 1], I32)
        junk = XT
        ywide = EW[:, :].rearrange("p r w n -> p (r w n)")
        ypair = view(ywide, 0, (T, 2, D))

        banks = [ctx.enter_context(nc.psum_tensor(f"bank{b}", [P, 512], F32)) for b in range(8)]

        bank_full = [sem(f"bank_full{b}") for b in range(8)]
        bank_free = [sem(f"bank_free{b}") for b in range(8)]
        x_landed = [sem(f"x_landed{t}") for t in range(T)]
        win_landed = [sem(f"win_landed{i}") for i in range(3)]
        first_landed = sem("first_landed")
        consts_landed = sem("consts_landed")
        gate_w_landed = sem("gate_w_landed")
        mla_w_landed = sem("mla_w_landed")
        dft_landed = sem("dft_landed")
        fnet_landed = sem("fnet_landed")
        wout_landed = sem("wout_landed")
        gf_landed = sem("gf_landed")
        krope_copied = sem("krope_copied")
        dve_chain = sem("dve_chain")
        act_chain = sem("act_chain")
        pool_chain = sem("pool_chain")
        angles_ready = sem("angles_ready")
        tables_ready = sem("tables_ready")
        squares_ready = sem("squares_ready")
        var_ready = sem("var_ready")
        guess_ready = sem("guess_ready")
        xn_ready = sem("xn_ready")
        gate_abs = sem("gate_abs")
        gate_log = sem("gate_log")
        decay_sum = sem("decay_sum")
        decay_exp = sem("decay_exp")
        gla_ready = sem("gla_ready")
        silu_exp = sem("silu_exp")
        latents_ready = sem("latents_ready")
        kr_rot = sem("kr_rot")
        q_rot = sem("q_rot")
        gatew_zero = sem("gatew_zero")
        fnetw_zero = sem("fnetw_zero")
        att_zero = sem("att_zero")
        gla_out = sem("gla_out")
        diag_zero = sem("diag_zero")
        q_diag_ready = sem("q_diag_ready")
        state_diag_ready = sem("state_diag_ready")
        keep_ready = sem("keep_ready")
        norm_ready = sem("norm_ready")
        av_done = sem("av_done")
        g2_landed = sem("g2_landed")
        x3_ready = sem("x3_ready")
        ov_tmp = sem("ov_tmp")
        held_done = sem("held_done")
        SQ2, SQ3 = T + 2 * T + GH, 3 * T + 2 * T + GH
        neg_max = sem("neg_max")
        x2_ready = sem("x2_ready")
        x2_stored = sem("x2_stored")
        logit_ready = sem("logit_ready")
        rexp_ready = sem("rexp_ready")
        picks_ready = sem("picks_ready")
        dest_ready = sem("dest_ready")
        list_filled = sem("list_filled")
        fill_ready = sem("fill_ready")
        scattered = sem("scattered")
        list_loaded = sem("list_loaded")
        idx_ready = sem("idx_ready")
        nmax_ready = sem("nmax_ready")
        xg_landed = [sem(f"xg_landed{s}") for s in range(2)]
        sel_ready = sem("sel_ready")
        gu_landed = [sem(f"gu_landed{s}") for s in range(FIRST)]
        dn_landed = [sem(f"dn_landed{s}") for s in range(FIRST)]
        xe_full = sem("xe_full")
        xe_ready = sem("xe_ready")
        gu_full = sem("gu_full")
        silu_done = sem("silu_done")
        hg_ready = sem("hg_ready")
        hT_full = sem("hT_full")
        hT_ready = sem("hT_ready")
        y_full = sem("y_full")
        y_ready = sem("y_ready")
        y_stored = [sem(f"y_stored{s}") for s in range(2)]
        ov_w = sem("ov_w")
        ov_list = sem("ov_list")
        ov_idx = sem("ov_idx")
        ov_x = sem("ov_x")
        ov_xt = sem("ov_xt")
        ov_xc = sem("ov_xc")
        ov_gu = sem("ov_gu")
        ov_silu = sem("ov_silu")
        ov_hg = sem("ov_hg")
        ov_hT = sem("ov_hT")
        ov_hc = sem("ov_hc")
        ov_y = sem("ov_y")
        ov_yc = sem("ov_yc")
        ov_stored = sem("ov_stored")
        moe_done = sem("moe_done")
        pair_landed = [[sem(f"pair_landed{t}_{r}") for r in range(2)] for t in range(T)]
        x3_gain = sem("x3_gain")
        root_ready = sem("root_ready")
        out_ready = sem("out_ready")
        out_stored = sem("out_stored")

        def open_bank(key):
            b, _, before, _ = PLAN[key]
            if before:
                nc.tensor.wait_ge(bank_free[b], before)
            return banks[b]

        def close_bank(ins, key):
            ins.then_inc(bank_full[PLAN[key][0]], 1)

        def filled(eng, key):
            b, full, _, _ = PLAN[key]
            eng.wait_ge(bank_full[b], full)
            return banks[b]

        def free_bank(ins, key):
            ins.then_inc(bank_free[PLAN[key][0]], 1)

        def drained(eng, key):
            b, _, _, after = PLAN[key]
            eng.wait_ge(bank_free[b], after)

        def linker(eng, chain):
            count = [0]

            def link(ins):
                count[0] += 1
                ins.then_inc(chain, 1)
                eng.wait_ge(chain, count[0])
            return link

        N_CONSTS = 12
        block = ctx.enter_context(nc.Block())

        @block.sync
        def _(sp):
            sp.dma_start(small[:, :], d["c_small"]).then_inc(first_landed, 16)
            sp.dma_start(posi[:, :],
                         d["positions"].rearrange("b (t p) -> p (b t)", p=P),
                         allow_slow_non_contiguous=True).then_inc(first_landed, 16)
            sp.dma_start(ident[:, :], d["c_ident"]).then_inc(first_landed, 16)
            sp.dma_start(gain1[:, :], d["norm1_g"][0].rearrange("(p c) -> p c", c=C)).then_inc(first_landed, 16)
            for t in range(T):
                sp.dma_start(X[:, t, :], x_v[:, t, :]).then_inc(x_landed[t], 16)
            sp.dma_start(w_in_sb[:, :, GQ:GV], w_in_v[:, :, GQ:GV]).then_inc(win_landed[1], 16)
            sp.dma_start(w_in_sb[:, :, GA:W_IN], w_in_v[:, :, GA:W_IN]).then_inc(win_landed[0], 16)
            sp.dma_start(w_in_sb[:, :, GV:GA], w_in_v[:, :, GV:GA]).then_inc(win_landed[2], 16)
            sp.wait_ge(gatew_zero, 2)
            for g in range(0, P, 32):
                sp.dma_start(wa[g:g + 16, 0, :], d["gla_wa_f"][0]).then_inc(gate_w_landed, 16)
                sp.dma_start(wa[g + 16:g + 32, 1, :], d["gla_wa_b"][0]).then_inc(gate_w_landed, 16)
            for dst, src in ((ba[:, 0:1], d["gla_ba_f"].rearrange("l n -> n l")),
                             (ba[:, 1:2], d["gla_ba_b"].rearrange("l n -> n l")),
                             (gainq[:, :], d["mla_q_norm_g"][0].rearrange("(p c) -> p c", c=2)),
                             (gainkv[:, :], d["mla_kv_norm_g"].rearrange("l n -> n l")),
                             (gain_gla[:, :], d["gla_norm_g"][0].partition_broadcast(P)),
                             (mask[:, :, :], d["c_mask"]),
                             (tri[:, :, :], d["c_tri"]),
                             (rank[:, :], d["c_rank"]),
                             (wr[:, :, 0:NG], d["moe_w_rg"][0].rearrange("(p c) n -> p c n", c=C)),
                             (wr[:, :, NG:NG + NE], d["moe_w_re"][0].rearrange("(p c) n -> p c n", c=C)),
                             (rbias[:, 0:NG], d["moe_b_rg"][0].partition_broadcast(P)),
                             (rbias[:, NG:], d["moe_b_re"][0].partition_broadcast(P))):
                sp.dma_start(dst, src).then_inc(consts_landed, 16)
            sp.dma_start(w_uq, d["mla_w_uq"][0].rearrange("(p c) n -> p c n", c=2)).then_inc(mla_w_landed, 16)
            sp.dma_start(w_ukv.rearrange("p a b -> p (a b)"), d["mla_w_ukv"][0]).then_inc(mla_w_landed, 16)
            for i in range(2):
                sp.dma_start(dft[:, i], d["c_dft"][i].rearrange("(t p) n -> p t n", p=P)).then_inc(dft_landed, 16)
            sp.wait_ge(fill_ready, 1)
            sp.dma_start(list_d.rearrange("(p n) o -> p (n o)", p=P), lfill[:, :]).then_inc(list_filled, 16)
            sp.wait_ge(fnetw_zero, 1)
            for g in range(4):
                r = slice(64 * (g % 2), 64 * (g % 2) + 64)
                sp.dma_start(fw[r, g // 2, r], d["fnet_w"][0, g]).then_inc(fnet_landed, 16)
            sp.dma_start(chan, d["c_chan"]).then_inc(fnet_landed, 16)
            drained(sp, "krT")
            for h in range(1, MH):
                sp.dma_start(kT[NOPE:QD, h, :], kT[NOPE:QD, 0, :]).then_inc(krope_copied, 16)
            drained(sp, ("fy", T - 1))
            sp.wait_ge(gla_out, 1)
            sp.dma_start(g2b, d["norm2_g"][0].partition_broadcast(P)).then_inc(g2_landed, 16)
            sp.dma_start(w_out_sb[:, 0:C // 2], w_out_v[:, 0:C // 2]).then_inc(wout_landed, 16)
            sp.dma_start(w_out_sb[:, C // 2:], w_out_v[:, C // 2:]).then_inc(wout_landed, 16)

            def load_gate_up(place, e):
                one = isinstance(e, int)
                for w, src in enumerate((w_gate_v, w_up_v)):
                    sp.dma_start(gu_at[place][:, w * C * DE:(w + 1) * C * DE],
                                 src[e] if one else src[e].rearrange("e p n -> p (e n)")).then_inc(gu_landed[place], 16)

            def load_down(place, e):
                one = isinstance(e, int)
                sp.dma_start(dn_at[place].rearrange("p (c n) -> p c n", c=2),
                             w_down_v[e] if one else w_down_v[e].rearrange("e p c n -> p (e c) n")).then_inc(dn_landed[place], 16)

            for h in range(MH):
                drained(sp, ("qT", h))
            for s in (2, 3):
                load_gate_up(s, s)
                load_down(s, s)
            for t in range(T):
                drained(sp, ("O", t))
            for s in (0, 1):
                load_gate_up(s, s)
                load_down(s, s)
            for t in range(T):
                if t == T - 1:
                    for u in range(T):
                        for n in range(2):
                            drained(sp, ("out", u, n))
                    load_gate_up(RING, RING)
                    load_down(RING, RING)
                sp.wait_ge(x2_ready, t + 1)
                sp.dma_start(x2_d[t * P:(t + 1) * P, :], MIX[:, t, :]).then_inc(x2_stored, 16)
            for t in range(T):
                drained(sp, ("Lf", t))
            load_gate_up(RING + 1, RING + 1)
            sp.wait_ge(scattered, 16 * 2 * T)
            for i in range(2):
                sp.dma_start(lst[:, i * BLOCK:(i + 1) * BLOCK],
                             list_d.rearrange("(e s) o -> e (s o)", e=NE)[:, 0:BLOCK]).then_inc(list_loaded, 16)
            sp.wait_ge(nmax_ready, 1)
            load_down(RING + 1, RING + 1)
            for s in range(RING):
                sp.wait_ge(gu_full, s + 1)
                load_gate_up(s, FIRST + s)
                sp.wait_ge(y_full, s + 1)
                load_down(s, FIRST + s)
            with sp.Fori(1, TURNS) as i:
                for s in range(RING):
                    e = i * RING + (FIRST + s)
                    sp.wait_ge(gu_full, i * RING + (FIRST + s - RING + 1))
                    load_gate_up(s, bass.ds(e, 1))
                    sp.wait_ge(y_full, i * RING + (FIRST + s - RING + 1))
                    load_down(s, bass.ds(e, 1))
            for e in range(FIRST + TURNS * RING, NE):
                sp.wait_ge(gu_full, e - RING + 1)
                load_gate_up((e - FIRST) % RING, e)
                sp.wait_ge(y_full, e - RING + 1)
                load_down((e - FIRST) % RING, e)
            sp.dma_start(gfb, d["final_norm_g"].partition_broadcast(P)).then_inc(gf_landed, 16)
            sp.wait_ge(nmax_ready, 1)
            sp.wait_ge(y_full, NE)
            with sp.If(sp.value_load(nmax[0:1, 0:1]) > BLOCK):
                with sp.Fori(0, NE) as e:
                    with sp.Fori(0, OVB) as k:
                        for q in range(2):
                            sp.wait_ge(held_done, e * (OVB * 3) + k * 3 + 1)
                            sp.dma_start(ovl[q * BLOCK:(q + 1) * BLOCK, 0:1],
                                         list_d[bass.ds(e * S + k * BLOCK, BLOCK), :]).then_inc(ov_list, 16)
                        for w, src in enumerate((w_gate_v, w_up_v)):
                            sp.wait_ge(ov_y, e * OVB + k + 1)
                            sp.dma_start(EW[:, 0, w], src[bass.ds(e, 1)].rearrange("e p n -> p (e n)")).then_inc(ov_w, 16)
                        sp.dma_start(EW[:, 0, 2].rearrange("p (c n) -> p c n", c=2),
                                     w_down_v[bass.ds(e, 1)].rearrange("e p c n -> p (e c) n")).then_inc(ov_w, 16)
            sp.wait_ge(moe_done, 1)
            for t in range(T):
                for r in range(2):
                    sp.dma_start(ypair[:, t, r], y_d[r * S + t * P:r * S + (t + 1) * P, :]).then_inc(pair_landed[t][r], 16)
            for t in range(T):
                sp.wait_ge(out_ready, t + 1)
                sp.dma_start(out_v[:, t, :], X[:, t, :]).then_inc(out_stored, 16)
            sp.wait_ge(out_stored, 16 * T)

        @block.tensor
        def _(pe):
            pe.wait_ge(first_landed, 64)
            for t in range(T):
                pe.wait_ge(xn_ready, t + 1)
                for c in range(C):
                    if t == 0:
                        open_bank(("xT", c))
                    mm = pe.transpose(banks[PLAN[("xT", c)][0]][:, t * P:(t + 1) * P], MIX[:, t, c:D:C], ident[:, :])
                    if t == T - 1:
                        close_bank(mm, ("xT", c))
            for c in range(C):
                drained(pe, ("xT", c))

            def by_feature(key, col, width):
                ps = open_bank(key)
                for c in range(C):
                    mm = pe.matmul(ps[0:width, :], w_in_sb[:, c, col:col + width], xnT[:, c, :],
                                   start=(c == 0), stop=(c == C - 1))
                close_bank(mm, key)

            def by_token(key, t, col, width):
                ps = open_bank(key)
                for c in range(C):
                    mm = pe.matmul(ps[:, 0:width], xnT[:, c, t * P:(t + 1) * P], w_in_sb[:, c, col:col + width],
                                   start=(c == 0), stop=(c == C - 1))
                close_bank(mm, key)

            pe.wait_ge(win_landed[1], 16)
            by_feature(("pT", 1), GQ, 128)
            by_feature(("pT", 2), GK, 128)
            pe.wait_ge(win_landed[0], 16)
            ps = open_bank(("pT", 0))
            for c in range(C):
                mm = pe.matmul(ps[32 * (c % 4):32 * (c % 4 + 1), :], w_in_sb[:, c, GA:GA + 32], xnT[:, c, :],
                               start=(c < 4), stop=(c >= 4))
            close_bank(mm, ("pT", 0))
            for t in range(T):
                by_token(("ckr", t), t, CKV, 160)
                by_token(("ucq", t), t, FU, 512)
                if t == 0:
                    pe.wait_ge(gate_w_landed, 16 * 8)
                    drained(pe, ("pT", 0))
                    for dd in range(2):
                        ps = open_bank(("z", dd))
                        close_bank(pe.matmul(ps[:, :], wa[:, dd, :], gaT[:, :], start=True, stop=True), ("z", dd))
            pe.wait_ge(win_landed[2], 16)
            for t in range(T):
                by_token(("vg", t), t, GV, 512)

            pe.wait_ge(latents_ready, 8)
            ps = open_bank("ckvT")
            for t in range(T):
                mm = pe.transpose(ps[:, t * P:(t + 1) * P], ckr[:, t, 0:128], ident[:, :])
            close_bank(mm, "ckvT")
            for c in range(2):
                ps = open_bank(("cqT", c))
                for t in range(T):
                    mm = pe.transpose(ps[:, t * P:(t + 1) * P], ucq[:, t, 256 + c:512:2], ident[:, :])
                close_bank(mm, ("cqT", c))
            drained(pe, "ckvT")
            pe.wait_ge(mla_w_landed, 32)
            for h in range(0, MH, 2):
                ps = open_bank(("kT", h))
                for u in range(2):
                    mm = pe.matmul(ps[NOPE * u:NOPE * (u + 1), :], w_ukv[:, h + u, 0:NOPE], ckvT, start=True, stop=True)
                close_bank(mm, ("kT", h))
            for t in range(T):
                ps = open_bank(("V", t))
                close_bank(pe.matmul(ps[:, :], ckvT[:, t * P:(t + 1) * P], w_ukv[:, :, NOPE:],
                                     start=True, stop=True), ("V", t))
            pe.wait_ge(kr_rot, 1)
            ps = open_bank("krT")
            for t in range(T):
                mm = pe.transpose(ps[0:QD, t * P:(t + 1) * P], krp[:, t, :], ident[:, :])
            close_bank(mm, "krT")
            drained(pe, ("cqT", 0))
            drained(pe, ("cqT", 1))
            for t in range(T):
                for n in range(2):
                    ps = open_bank(("q", t, n))
                    for c in range(2):
                        mm = pe.matmul(ps[:, 0:384], cqT[:, c, t * P:(t + 1) * P], w_uq[:, c, n * 384:(n + 1) * 384],
                                       start=(c == 0), stop=(c == 1))
                    close_bank(mm, ("q", t, n))

            pe.wait_ge(dft_landed, 32)
            for i in range(4):
                ps = open_bank(("AB", i))
                for t in range(T):
                    mm = pe.matmul(ps[:, 0:FREQ], ucq[:, t, (i % 2) * P:(i % 2 + 1) * P], dft[:, i // 2, t, :],
                                   start=(t == 0), stop=(t == T - 1))
                close_bank(mm, ("AB", i))
            pe.wait_ge(fnet_landed, 80)
            ps = open_bank("M")
            for i in range(2):
                for blk in range(2):
                    at = (2 * i + blk) * P
                    mm = pe.matmul(ps[:, at:at + P], chan[:, i, :], fw[:, blk, :], start=True, stop=True)
            close_bank(mm, "M")
            for i in range(4):
                drained(pe, ("AB", i))
            drained(pe, "M")
            for t in range(T):
                ps = open_bank(("fy", t))
                for blk in range(2):
                    for i in range(2):
                        mm = pe.matmul(ps[:, blk * P:(blk + 1) * P], AB[:, i, blk, t * P:(t + 1) * P],
                                       fM[:, i, blk, :], start=(i == 0), stop=(i == 1))
                close_bank(mm, ("fy", t))

            pe.wait_ge(gla_ready, 6)
            for dd in range(2):
                ps = open_bank(("kendT", dd))
                for t in range(T):
                    mm = pe.transpose(ps[:, t * P:(t + 1) * P], gexp[:, dd, 0, t * P:(t + 1) * P], ident[:, :])
                close_bank(mm, ("kendT", dd))
            for dd in range(2):
                drained(pe, ("kendT", dd))
                for odd in range(2):
                    ps = open_bank(("kv", dd, odd))
                    rows = slice(CHUNK * odd, CHUNK * odd + CHUNK)
                    for t in range(T):
                        for h in range(GH):
                            mm = pe.matmul(ps[GDK * h:GDK * (h + 1), t * GDV:(t + 1) * GDV],
                                           kend_tok[rows, dd, t, GDK * h:GDK * (h + 1)],
                                           vg[rows, t, GDV * h:GDV * (h + 1)], start=True, stop=True)
                    close_bank(mm, ("kv", dd, odd))
            pe.wait_ge(q_diag_ready, 2 * GH)
            for t in range(T):
                for dd in range(2):
                    ps = open_bank(("att", t, dd))
                    close_bank(pe.matmul(ps[:, :], kinv[:, dd, t * P:(t + 1) * P],
                                         q_diag[:, dd, t].rearrange("p h n -> p (h n)"), start=True, stop=True),
                               ("att", t, dd))
            pe.wait_ge(q_rot, T)
            for h in range(MH):
                ps = open_bank(("qT", h))
                for t in range(T):
                    mm = pe.transpose(ps[0:QD, t * P:(t + 1) * P], qs[:, t, h, :], ident[:, :])
                close_bank(mm, ("qT", h))
            pe.wait_ge(state_diag_ready, 2 * GH)
            for t in range(T):
                drained(pe, ("att", t, 0))
                drained(pe, ("att", t, 1))
                ps = open_bank(("o", t))
                for h in range(GH):
                    pe.matmul(ps[:, h * GDV:(h + 1) * GDV], att[:, t, h, :], vg[:, t, GDV * h:GDV * (h + 1)],
                              start=(h == 0), stop=False, skip_group_check=True)
                for dd in range(2):
                    for u in range(2):
                        n = 2 * t + u
                        if n != (0 if dd == 0 else NCH - 1):
                            mm = pe.matmul(ps[CHUNK * u:CHUNK * (u + 1), 0:GH * GDV],
                                           qdec[:, dd, n * CHUNK:(n + 1) * CHUNK],
                                           state_diag[:, dd, n].rearrange("p h v -> p (h v)"),
                                           start=False, stop=False, skip_group_check=True)
                close_bank(mm, ("o", t))

            pe.wait_ge(krope_copied, 16 * (MH - 1))
            for h in range(0, MH, 2):
                drained(pe, ("kT", h))
            for h in range(MH):
                drained(pe, ("qT", h))
            for t in range(T):
                drained(pe, ("V", t))
            for kind, i in attention_order():
                if kind == "S":
                    ps = open_bank(("S", i))
                    tq, h = i // MH, i % MH
                    close_bank(pe.matmul(ps[:, :], qT[0:QD, h, tq * P:(tq + 1) * P], kT[0:QD, h, :],
                                         start=True, stop=True), ("S", i))
                elif kind == "mT":
                    if i == 0:
                        pe.wait_ge(gla_out, 1)
                        for t in range(T):
                            drained(pe, ("fy", t))
                    ps = open_bank(("mT", i))
                    for t in range(T):
                        mm = pe.transpose(ps[:, t * P:(t + 1) * P], MIX[:, t, i * P:(i + 1) * P], ident[:, :])
                    close_bank(mm, ("mT", i))
                elif kind == "PT":
                    pe.wait_ge(norm_ready, i + 1)
                    ps = open_bank(("PT", i))
                    for kc in range(T):
                        mm = pe.transpose(ps[:, kc * P:(kc + 1) * P], probs[:, i % 4, kc * P:(kc + 1) * P], ident[:, :])
                    close_bank(mm, ("PT", i))
                else:
                    tq, hp = i // 4, i % 4
                    if hp == 0:
                        ps_o = open_bank(("O", tq))
                    drained(pe, ("PT", 2 * i))
                    drained(pe, ("PT", 2 * i + 1))
                    for kc in range(T):
                        for u in range(2):
                            h = 2 * hp + u
                            mm = pe.matmul(ps_o[MV * u:MV * (u + 1), hp * P:(hp + 1) * P],
                                           V[:, kc, h * MV:(h + 1) * MV],
                                           probsT[:, (2 * i + u) % 4, kc * P:(kc + 1) * P],
                                           start=(kc == 0), stop=(kc == T - 1))
                    mm.then_inc(av_done, 1)

            for t in range(T):
                drained(pe, ("O", t))
            for c in range(4):
                drained(pe, ("mT", c))
            pe.wait_ge(wout_landed, 32)
            pe.wait_ge(consts_landed, 16 * N_CONSTS)
            for step in OUT_ORDER:
                kind, t = step[0:2]
                if kind == "out":
                    n = step[2]
                    ps = open_bank(step)
                    for c in range(C):
                        mm = pe.matmul(ps[:, :], xnT[:, c, t * P:(t + 1) * P], w_out_sb[:, c, n * 512:(n + 1) * 512],
                                       start=(c == 0), stop=(c == C - 1))
                    close_bank(mm, step)
                elif kind == "T":
                    pe.wait_ge(x2_ready, t + 1)
                    for q in range(2):
                        ps = open_bank(("x2T", t, q))
                        for j in range(4):
                            c = 4 * q + j
                            mm = pe.transpose(ps[:, j * P:(j + 1) * P], MIX[:, t, c * P:(c + 1) * P], ident[:, :])
                        close_bank(mm, ("x2T", t, q))
                elif kind == "Lf":
                    drained(pe, ("x2T", t, 0))
                    drained(pe, ("x2T", t, 1))
                    ps = open_bank(step)
                    for c in range(C):
                        half = slice(64 * (c % 2), 64 * (c % 2) + 64)
                        mm = pe.matmul(ps[half, 0:P], wr[:, c, :], xnT[:, c, t * P:(t + 1) * P],
                                       start=(c < 2), stop=(c >= C - 2))
                    close_bank(mm, step)
                elif kind == "L":
                    drained(pe, ("Lf", t))
                    ps = open_bank(step)
                    close_bank(pe.matmul(ps[:, 0:NG + NE], lf[:, t % 2], small[:, STACK:ONE_UP], start=True, stop=True), step)
                elif kind == "pick":
                    pe.wait_ge(sel_ready, t + 1)
                    if t == 0:
                        for i in range(T * MH - 3, T * MH):
                            drained(pe, ("S", i))
                    for c in range(C):
                        mm = pe.matmul(banks[c // 4][:, c % 4 * P:(c % 4 + 1) * P], MIX[:, t, c * P:(c + 1) * P],
                                       sel0[:, t].rearrange("p e s -> p (e s)"), start=(t == 0 and c % 4 == 0),
                                       stop=(t == T - 1 and c % 4 == 3), skip_group_check=True)
                        if t == T - 1 and c % 4 == 3:
                            mm.then_inc(xe_full, 1)
                else:
                    pe.wait_ge(picks_ready, t + 1)
                    ps = open_bank(step)
                    for u in range(t + 1):
                        mm = pe.matmul(ps[:, 0:NE], tri[:, 1 if u < t else 0, :], mska[:, u, :],
                                       start=(u == 0), stop=(u == t))
                    close_bank(mm, step)
            ps = open_bank("count")
            for u in range(T):
                mm = pe.matmul(ps[:, 0:NE], tri[:, 1, :], mska[:, u, :], start=(u == 0), stop=(u == T - 1))
            close_bank(mm, "count")
            def select(half, buf):
                for j in range(4):
                    c = 4 * half + j
                    for t in range(T):
                        mm = pe.matmul(banks[half][:, j * P:(j + 1) * P], MIX[:, t, c * P:(c + 1) * P],
                                       sel[:, buf, t].rearrange("p e s -> p (e s)"), start=(t == 0), stop=(t == T - 1))
                return mm

            def tokens(buf, bank):
                for j in range(4):
                    mm = pe.transpose(banks[bank][:, j * P:(j + 1) * P], xg[buf][:, j * P:(j + 1) * P], ident[:, :])
                return mm

            def gate_up(place, par, buf):
                bank = banks[2 + par]
                wv = gu_at[place].rearrange("p (w c n) -> p w c n", w=2, c=C)
                for c in range(C):
                    for m in range(2):
                        mm = pe.matmul(bank[BLOCK * m:BLOCK * (m + 1), 0:2 * P].rearrange("p (w n) -> p w n", w=2),
                                       xeT[:, buf, c, par * BLOCK:(par + 1) * BLOCK],
                                       wv[:, :, c, m * P:(m + 1) * P], start=(c == 0), stop=(c == C - 1))
                return mm

            def transpose_h(par):
                return pe.transpose(banks[6 + par][:, 0:P], hg[:, par], ident[:, :])

            def down(place, par):
                bank = banks[4 + par]
                wv = dn_at[place].rearrange("p (c n) -> p c n", c=2)
                for m in range(2):
                    for q in range(2):
                        mm = pe.matmul(bank[BLOCK * q:BLOCK * (q + 1), :], hT[:, par, m, :],
                                       wv[:, m, q * 512:(q + 1) * 512], start=(m == 0), stop=(m == 1))
                return mm

            def expert(e, r, pick, turns, place, loads, prev, prev_loads):
                known = isinstance(e, int)
                par = r % 2
                pe.wait_ge(gu_landed[place], loads * 32)
                pe.wait_ge(xe_ready, e + (2 - par))
                if not (known and e < 2):
                    pe.wait_ge(hg_ready, e - 1)
                gate_up(place, par, r // 2).then_inc(gu_full, 1)
                if known and e == 0:
                    pe.wait_ge(list_loaded, 32)
                    ps = open_bank("listT")
                    close_bank(pe.transpose(ps[:, 0:NE], lst, ident[0:NE, 0:NE]), "listT")
                if not (known and e >= NE - 2):
                    pe.wait_ge(xe_ready, e + 1)
                    if pick:
                        pe.wait_ge(sel_ready, turns)
                        select(par, 1 - r // 2).then_inc(xe_full, 1)
                    else:
                        pe.wait_ge(xg_landed[par], turns * 16)
                        tokens(par, par).then_inc(xe_full, 1)
                if not (known and e < 1):
                    last_down(e - 1, prev, prev_loads, 1 - par)
                pe.wait_ge(hg_ready, e + 1)
                if not (known and e < 2):
                    pe.wait_ge(hT_ready, e - 1)
                if known and e == 0:
                    drained(pe, "listT")
                transpose_h(par).then_inc(hT_full, 1)

            def last_down(e, place, loads, par):
                pe.wait_ge(dn_landed[place], loads * 16)
                pe.wait_ge(hT_ready, e + 1)
                if not (isinstance(e, int) and e < 2):
                    pe.wait_ge(y_ready, e - 1)
                down(place, par).then_inc(y_full, 1)

            def place(e):
                return (e, 1) if e < FIRST else ((e - FIRST) % RING, (e - FIRST) // RING + 2)

            def known_expert(e):
                nxt = e // 2 + 1
                expert(e, e % 4, picked(nxt), picks(nxt) + T - 1 if picked(nxt) else nxt + 1 - picks(nxt), *place(e), *place(e - 1))

            drained(pe, "count")
            for t in range(T):
                drained(pe, ("pos", t))
                drained(pe, ("L", t))
            for e in range(FIRST + RING):
                known_expert(e)
            with pe.Fori(1, TURNS) as i:
                for s in range(RING):
                    e = FIRST + s
                    expert(i * RING + e, e % 4, True, i * (RING // 2) + (picks(e // 2 + 1) + T - 1),
                           s, i + 2, (s - 1) % RING, i + (2 if s else 1))
            for e in range(FIRST + TURNS * RING, NE):
                known_expert(e)
            last_down(NE - 1, *place(NE - 1), (NE - 1) % 2)

            pe.wait_ge(nmax_ready, 1)
            pe.wait_ge(y_ready, NE)
            with pe.If(pe.value_load(nmax[0:1, 0:1]) > BLOCK):
                pe.nop().then_inc(ov_y, 1)
                with pe.Fori(0, NE * OVB) as n:
                    pe.wait_ge(ov_x, n * 16 + 16)
                    tokens(0, 0).then_inc(ov_xt, 1)
                    pe.wait_ge(ov_w, n * 48 + 48)
                    pe.wait_ge(ov_xc, n + 1)
                    gate_up(0, 0, 0).then_inc(ov_gu, 1)
                    pe.wait_ge(ov_hg, n + 1)
                    transpose_h(0).then_inc(ov_hT, 1)
                    pe.wait_ge(ov_hc, n + 1)
                    down(0, 0).then_inc(ov_y, 1)

        @block.scalar
        def _(act):
            link = linker(act, act_chain)
            norms = [0]

            def root_guess(dst, src):
                norms[0] += 1
                act.wait_ge(var_ready, norms[0])
                link(act.activation(dst, src, ACT.Ln))
                act.activation(dst, dst, ACT.Exp, scale=-0.5).then_inc(guess_ready, 1)

            act.preload_act_table_set("natural_log_exp_and_others")
            for t in range(T):
                act.wait_ge(x_landed[t], 16)
                act.activation(junk[:, 0:D], X[:, t, :], ACT.Square, accum_out=stat[:, t:t + 1]).then_inc(squares_ready, 1)
                act.wait_ge(squares_ready, t + 1)
                if t >= 1:
                    root_guess(stat[:, 7 + t:8 + t], stat[:, 3 + t:4 + t])
            root_guess(stat[:, 11:12], stat[:, 7:8])
            for c in range(0, C, 2):
                ps = filled(act, ("xT", c))
                free_bank(act.activation(xnT[:, c, :], ps[:, :], ACT.Copy, scale=gain1[:, c:c + 1]), ("xT", c))
            act.preload_act_table_set("silu_and_others")
            act.wait_ge(angles_ready, 1)
            act.activation(ropet[:, 0], ropet[:, 0], ACT.Sin).then_inc(tables_ready, 1)
            act.activation(ropet[:, 1], ropet[:, 1], ACT.Sin).then_inc(tables_ready, 1)
            act.preload_act_table_set("natural_log_exp_and_others")
            ps = filled(act, ("pT", 0))
            free_bank(act.activation(gaT[:, :], ps[:, :], ACT.Copy), ("pT", 0))

            def copy_ckr(t):
                ps = filled(act, ("ckr", t))
                free_bank(act.activation(ckr[:, t, :], ps[:, 0:160], ACT.Copy), ("ckr", t))
                drained(act, ("ckr", t))
                act.activation(squares_out[:, 0:128], ckr[:, t, 0:128], ACT.Square, accum_out=stat[:, 20 + t:21 + t]).then_inc(squares_ready, 1)
                act.wait_ge(squares_ready, T + 2 * t + 1)
                drained(act, ("ucq", t))
                act.activation(squares_out, ucq[:, t, 256:512], ACT.Square, accum_out=stat[:, 16 + t:17 + t]).then_inc(squares_ready, 1)
                act.wait_ge(squares_ready, T + 2 * t + 2)

            copy_ckr(0)
            for dd in range(2):
                act.wait_ge(gate_abs, dd + 1)
                link(act.activation(gexp[:, dd, 0], gexp[:, dd, 0], ACT.Exp))
                act.activation(gexp[:, dd, 1], gexp[:, dd, 0], ACT.Ln, bias=1.0).then_inc(gate_log, 1)
            copy_ckr(1)
            for dd in range(2):
                act.wait_ge(decay_sum, dd + 1)
                act.activation(gexp[:, dd, 0], cum[:, dd], ACT.Exp, scale=1.0 / TAU).then_inc(decay_exp, 1)
                act.activation(gexp[:, dd, 1], cum[:, dd], ACT.Exp, scale=-1.0 / TAU).then_inc(decay_exp, 1)
                act.activation(dec[:, dd], tot[:, dd], ACT.Exp, scale=1.0 / TAU).then_inc(decay_exp, 1)
            copy_ckr(2)
            copy_ckr(3)
            root_guess(stat[:, 32:40], stat[:, 24:32])
            for t in range(T):
                ps = filled(act, ("vg", t))
                free_bank(act.activation(vg[:, t, :], ps[:, :], ACT.Copy), ("vg", t))
            for t in range(T):
                drained(act, ("vg", t))
            act.activation(sgt, vg[:, :, 256:512], ACT.Exp, scale=-1.0).then_inc(silu_exp, 1)
            ps = filled(act, "ckvT")
            act.wait_ge(consts_landed, 16 * N_CONSTS)
            free_bank(act.activation(ckvT, ps[:, :], ACT.Copy, scale=gainkv[:, 0:1]), "ckvT")
            for h in range(0, MH, 2):
                ps = filled(act, ("kT", h))
                free_bank(act.activation(kT[0:NOPE, h, :], ps[0:NOPE, :], ACT.Copy), ("kT", h))
            for t in range(0, T, 2):
                ps = filled(act, ("V", t))
                free_bank(act.activation(V[:, t, :], ps[:, :], ACT.Copy), ("V", t))
            ps = filled(act, "krT")
            free_bank(act.activation(kT[NOPE:QD, 0, :], ps[NOPE:QD, :], ACT.Copy), "krT")
            for t in range(T):
                for n in range(2):
                    ps = filled(act, ("q", t, n))
                    free_bank(act.activation(qs[:, t, 4 * n:4 * n + 4].rearrange("p h w -> p (h w)"), ps[:, 0:384],
                                             ACT.Copy, scale=float(QD) ** -0.5), ("q", t, n))
            for i in (0, 2):
                ps = filled(act, ("AB", i))
                act.activation(AB[:, i // 2, i % 2, FREQ:], ps[:, S - FREQ:0:-1], ACT.Copy,
                               scale=1.0 if i < 2 else -1.0)
                free_bank(act.activation(AB[:, i // 2, i % 2, 0:FREQ], ps[:, 0:FREQ], ACT.Copy), ("AB", i))
            ps = filled(act, "M")
            free_bank(act.activation(fM.rearrange("p a b n -> p (a b n)"), ps[:, :], ACT.Copy), "M")
            for t in range(T):
                ps = filled(act, ("fy", t))
                free_bank(act.activation(MIX[:, t, 256:512], ps[:, 0:256], ACT.Copy), ("fy", t))
            act.wait_ge(diag_zero, 1)
            act.wait_ge(gla_ready, 6)
            for dd in range(2):
                for h in range(GH):
                    rows = slice(GDK * h, GDK * (h + 1))
                    act.activation(q_diag[rows, dd, :, h, :], qdec[rows, dd].rearrange("p (t n) -> p t n", t=T),
                                   ACT.Copy).then_inc(q_diag_ready, 1)
            act.wait_ge(diag_zero, 2)
            for dd in range(2):
                drained(act, ("kv", dd, 0))
                drained(act, ("kv", dd, 1))
                ns = slice(1, NCH) if dd == 0 else slice(0, NCH - 1)
                for h in range(GH):
                    rows = slice(GDK * h, GDK * (h + 1))
                    act.activation(state_diag[rows, dd, ns, h, :], state[rows, dd, ns, :],
                                   ACT.Copy).then_inc(state_diag_ready, 1)
            for h in range(0, MH, 2):
                ps = filled(act, ("qT", h))
                free_bank(act.activation(qT[0:QD, h, :], ps[0:QD, :], ACT.Copy), ("qT", h))
            for t in range(T):
                ps = filled(act, ("o", t))
                act.activation(osq[:, t], ps[:, 0:GH * GDV], ACT.Square).then_inc(squares_ready, 1)
            root_guess(rgla[:, 1], rgla[:, 0])
            for i in range(T * MH + 3):
                if i < T * MH:
                    ps = filled(act, ("S", i))
                    act.wait_ge(neg_max, i + 1)
                    if i >= 4:
                        act.wait_ge(bank_full[PLAN[("PT", i - 4)][0]], PLAN[("PT", i - 4)][1])
                    free_bank(act.activation(probs[:, i % 4], ps[:, :], ACT.Exp, bias=nm[:, i:i + 1],
                                             accum_out=rs[:, i:i + 1]), ("S", i))
                if i == 2:
                    for c in range(0, 4, 2):
                        ps = filled(act, ("mT", c))
                        free_bank(act.activation(xnT[:, c, :], ps[:, :], ACT.Copy), ("mT", c))
                j = i - 3
                if j >= 0:
                    ps = filled(act, ("PT", j))
                    if j >= 4:
                        act.wait_ge(av_done, (j - 4) // 2 + 1)
                    free_bank(act.activation(probsT[:, j % 4], ps[:, :], ACT.Copy), ("PT", j))
            for step in OUT_ORDER:
                kind, t = step[0:2]
                if kind == "out":
                    n = step[2]
                    drained(act, step)
                    act.activation(sqj[:, n * 512:(n + 1) * 512], X[:, t, n * 512:(n + 1) * 512], ACT.Square,
                                   scale=float(D) ** -0.5, accum_out=rn2[:, t, 4 * n:4 * n + 1]).then_inc(squares_ready, 1)
                    act.wait_ge(squares_ready, SQ2 + 2 * t + n + 1)
                    if n == 1:
                        root_guess(rn2[:, t, 2:3], rn2[:, t, 1:2])
                elif kind == "T":
                    for q in range(1 if t == T - 1 else 2):
                        ps = filled(act, ("x2T", t, q))
                        free_bank(act.activation(xnT[:, 4 * q:4 * q + 4, t * P:(t + 1) * P],
                                                 ps[:, :].rearrange("p (c n) -> p c n", c=4), ACT.Copy), ("x2T", t, q))
                elif kind == "Lf":
                    ps = filled(act, step)
                    if t >= 2:
                        act.wait_ge(bank_full[PLAN[("L", t - 2)][0]], PLAN[("L", t - 2)][1])
                    free_bank(act.activation(lf[:, t % 2], ps[:, 0:P], ACT.Copy), step)
                elif kind == "pos":
                    act.wait_ge(logit_ready, 2 * t + 1)
                    act.activation(rt[:, t, 1, 0:NG], lg[:, t, 0:NG], ACT.Exp, bias=rt[:, t, 0, 3:4],
                                   accum_out=rt[:, t, 0, 0:1]).then_inc(rexp_ready, 1)
                    act.wait_ge(logit_ready, 2 * t + 2)
                    act.activation(rt[:, t, 0, 4:5], rt[:, t, 0, 5:6], ACT.Exp).then_inc(rexp_ready, 1)
            act.preload_act_table_set("silu_and_others")

            def expert(e, slot):
                act.wait_ge(gu_full, e + 1)
                if not (isinstance(e, int) and e < 2):
                    act.wait_ge(hg_ready, e - 1)
                act.activation(hs[:, slot % 2], banks[2 + slot % 2][:, 0:P], ACT.Silu).then_inc(silu_done, 1)

            def copy_gathered(buf, par):
                return act.activation(xeT[:, buf, :, par * BLOCK:(par + 1) * BLOCK].rearrange("p (h j) s -> p h j s", h=2),
                                      banks[par][:, :].rearrange("p (j h s) -> p h j s", j=4, h=2), ACT.Copy)

            def copy_tokens(k, half, buf, pick):
                act.wait_ge(xe_full, k + 1)
                if pick:
                    ins = act.activation(xeT[:, buf, 4 * half:4 * half + 4],
                                         banks[half][:, :].rearrange("p (j s) -> p j s", j=4), ACT.Copy)
                else:
                    ins = copy_gathered(buf, half)
                ins.then_inc(xe_ready, 1)

            for half in range(2):
                copy_tokens(half, half, 0, True)

            def step(e, s, pick):
                expert(e, s)
                if not (isinstance(e, int) and e >= NE - 2):
                    copy_tokens(e + 2, s % 2, 1 - s // 2, pick)

            for e in range(2 * RING):
                step(e, e % RING, picked(e // 2 + 1))
            with act.Fori(2, NE // RING - 1) as i:
                for s in range(RING):
                    step(i * RING + s, s, True)
            for e in range(NE - RING, NE):
                step(e, e % RING, picked(e // 2 + 1))
            act.wait_ge(nmax_ready, 1)
            act.wait_ge(y_ready, NE)
            with act.If(act.value_load(nmax[0:1, 0:1]) > BLOCK):
                with act.Fori(0, NE * OVB) as n:
                    act.wait_ge(ov_xt, n + 1)
                    copy_gathered(0, 0).then_inc(ov_xc, 1)
                    act.wait_ge(ov_gu, n + 1)
                    act.activation(hs[:, 0], banks[2][:, 0:P], ACT.Silu).then_inc(ov_silu, 1)
            act.preload_act_table_set("natural_log_exp_and_others")
            def finish(t):
                act.wait_ge(root_ready, t + 1)
                act.wait_ge(x3_gain, t + 1)
                act.activation(X[:, t, :], MIX[:, t, :], ACT.Copy, scale=stat[:, 56 + t:57 + t]).then_inc(out_ready, 1)

            for t in range(T):
                act.wait_ge(x3_ready, t + 1)
                act.activation(sqj, X[:, t, :], ACT.Square, accum_out=stat[:, 48 + t:49 + t]).then_inc(squares_ready, 1)
                act.wait_ge(squares_ready, SQ3 + t + 1)
                root_guess(stat[:, 56 + t:57 + t], stat[:, 52 + t:53 + t])
                if 1 <= t < T - 1:
                    finish(t - 1)
            finish(T - 2)
            finish(T - 1)

        @block.vector
        def _(dve):
            link = linker(dve, dve_chain)
            norms = [0]

            def variance(dst, ss, n):
                dve.tensor_scalar(dst, ss, 1.0 / n, EPS, ALU.mult, ALU.add).then_inc(var_ready, 1)
                norms[0] += 1

            def refine(guess, var, tmp, count=None):
                dve.wait_ge(guess_ready, count or norms[0])
                link(dve.tensor_tensor(tmp, guess, guess, ALU.mult))
                link(dve.scalar_tensor_tensor(tmp, tmp, -0.5, var, ALU.mult, ALU.mult))
                link(dve.scalar_tensor_tensor(guess, tmp, 1.5, guess, ALU.add, ALU.mult))

            dve.wait_ge(first_landed, 64)
            ang = ropet[:, 0]
            kk = ropet[:, 1]
            link(dve.tensor_copy(posf[:, :], posi[:, :]))
            link(dve.tensor_tensor(ang, posf[:, :].unsqueeze(2).to_broadcast([P, T, HALF]),
                                   small[:, 49:65].unsqueeze(1).to_broadcast([P, T, HALF]), ALU.mult))
            link(dve.tensor_scalar(kk, ang, float(1.0 / (2.0 * np.pi)), MAGIC, ALU.mult, ALU.add))
            link(dve.tensor_scalar(kk, kk, MAGIC, None, ALU.subtract))
            for part in TWO_PI_PARTS:
                link(dve.scalar_tensor_tensor(ang, kk, -part, ang, ALU.mult, ALU.add))
            link(dve.tensor_scalar(ang, ang, 3.1415925, -3.1415925, ALU.min, ALU.max))
            link(dve.scalar_tensor_tensor(kk, ang, -1.0, ang, ALU.mult, ALU.min))
            dve.tensor_scalar(kk, kk, float(np.pi / 2), None, ALU.add).then_inc(angles_ready, 1)

            for t in range(T):
                for u in ((0, 1) if t == 0 else (t + 1,) if t < T - 1 else ()):
                    dve.wait_ge(squares_ready, u + 1)
                    variance(stat[:, 4 + u:5 + u], stat[:, u:u + 1], D)
                    dve.wait_ge(var_ready, norms[0])
                refine(stat[:, 8 + t:9 + t], stat[:, 4 + t:5 + t], stat[:, 12 + t:13 + t], t + 1)
                dve.wait_ge(x_landed[t], 16)
                dve.tensor_scalar(MIX[:, t, :], X[:, t, :], stat[:, 8 + t:9 + t], None, ALU.mult).then_inc(xn_ready, 1)
            for c in range(1, C, 2):
                ps = filled(dve, ("xT", c))
                free_bank(dve.tensor_scalar(xnT[:, c, :], ps[:, :], gain1[:, c:c + 1], None, ALU.mult), ("xT", c))
            ps = filled(dve, ("pT", 1))
            free_bank(dve.tensor_scalar(qg, ps[:, :], float(GDK) ** -0.5, None, ALU.mult), ("pT", 1))
            ps = filled(dve, ("pT", 2))
            free_bank(dve.tensor_copy(kg, ps[:, :]), ("pT", 2))

            def copy_ucq(t):
                ps = filled(dve, ("ucq", t))
                free_bank(dve.tensor_copy(ucq[:, t, :], ps[:, :]), ("ucq", t))

            copy_ucq(0)
            dve.wait_ge(consts_landed, 16 * N_CONSTS)
            for dd in range(2):
                ps = filled(dve, ("z", dd))
                free_bank(dve.tensor_scalar(la[:, dd], ps[:, :], ba[:, dd:dd + 1], None, ALU.add), ("z", dd))
                drained(dve, ("z", dd))
                dve.scalar_tensor_tensor(gexp[:, dd, 0], la[:, dd], -1.0, la[:, dd], ALU.mult, ALU.min).then_inc(gate_abs, 1)
            dve.wait_ge(keep_ready, 1)
            for dd in range(2):
                dve.wait_ge(gate_log, dd + 1)
                link(dve.scalar_tensor_tensor(la[:, dd], la[:, dd], 0.0, gexp[:, dd, 1], ALU.min, ALU.subtract))
                link(dve.tensor_tensor_scan(cum[:, dd], keep, la[:, dd], 0.0, ALU.mult, ALU.add))
                ends = cum[:, dd].rearrange("p (n s) -> p n s", s=CHUNK)[:, :, CHUNK - 1]
                if dd == 0:
                    dve.tensor_copy(tot[:, dd], ends).then_inc(decay_sum, 1)
                else:
                    link(dve.tensor_copy(tot[:, dd], ends))
                    link(dve.tensor_tensor(la[:, dd], la[:, dd], cum[:, dd], ALU.subtract))
                    dve.tensor_tensor(cum[:, dd].rearrange("p (n s) -> p n s", s=CHUNK),
                                      la[:, dd].rearrange("p (n s) -> p n s", s=CHUNK),
                                      tot[:, dd].unsqueeze(2).to_broadcast([P, NCH, CHUNK]), ALU.add).then_inc(decay_sum, 1)
            copy_ucq(1)
            for dd in range(2):
                dve.wait_ge(decay_exp, 3 * dd + 3)
                if dd == 0:
                    drained(dve, ("pT", 1))
                    drained(dve, ("pT", 2))
                dve.tensor_tensor(qdec[:, dd], qg, gexp[:, dd, 0], ALU.mult).then_inc(gla_ready, 1)
                dve.tensor_tensor(kinv[:, dd], kg, gexp[:, dd, 1], ALU.mult).then_inc(gla_ready, 1)
                dve.wait_ge(gla_ready, 3 * dd + 2)
                dve.tensor_tensor(gexp[:, dd, 0].rearrange("p (n s) -> p n s", s=CHUNK),
                                  kinv[:, dd].rearrange("p (n s) -> p n s", s=CHUNK),
                                  dec[:, dd].unsqueeze(2).to_broadcast([P, NCH, CHUNK]), ALU.mult).then_inc(gla_ready, 1)
            copy_ucq(2)
            copy_ucq(3)
            dve.wait_ge(squares_ready, T + 8)
            link(dve.tensor_scalar(stat[:, 24:28], stat[:, 16:20], 1.0 / 256, EPS, ALU.mult, ALU.add))
            variance(stat[:, 28:32], stat[:, 20:24], 128)
            dve.wait_ge(var_ready, norms[0])
            refine(stat[:, 32:40], stat[:, 24:32], stat[:, 40:48])
            for t in range(T):
                drained(dve, ("ucq", t))
                dve.tensor_scalar(ucq[:, t, 256:512], ucq[:, t, 256:512], stat[:, 32 + t:33 + t], None,
                                  ALU.mult).then_inc(latents_ready, 1)
                dve.tensor_scalar(ckr[:, t, 0:128], ckr[:, t, 0:128], stat[:, 36 + t:37 + t], None,
                                  ALU.mult).then_inc(latents_ready, 1)
            for c in range(2):
                ps = filled(dve, ("cqT", c))
                free_bank(dve.tensor_scalar(cqT[:, c, :], ps[:, :], gainq[:, c:c + 1], None, ALU.mult), ("cqT", c))
            for h in range(0, MH, 2):
                ps = filled(dve, ("kT", h))
                free_bank(dve.tensor_copy(kT[0:NOPE, h + 1, :], ps[NOPE:2 * NOPE, :]), ("kT", h))
            for t in range(1, T, 2):
                ps = filled(dve, ("V", t))
                free_bank(dve.tensor_copy(V[:, t, :], ps[:, :]), ("V", t))
            gg = vg[:, :, 256:512]
            dve.wait_ge(silu_exp, 1)
            link(dve.tensor_scalar(sgt, sgt, 1.0, None, ALU.add))
            link(dve.reciprocal(sgt, sgt))
            link(dve.tensor_tensor(gg, gg, sgt, ALU.mult))
            for t in range(T):
                gt = vg[:, t, 256:512].rearrange("p (h v) -> p h v", h=GH)
                link(dve.tensor_tensor(gt, gt, gain_gla[:, :].unsqueeze(1).to_broadcast([P, GH, GDV]), ALU.mult))
            for i in (1, 3):
                ps = filled(dve, ("AB", i))
                dve.tensor_scalar(AB[:, i // 2, i % 2, FREQ:], ps[:, S - FREQ:0:-1], 1.0 if i < 2 else -1.0, None, ALU.mult)
                free_bank(dve.tensor_copy(AB[:, i // 2, i % 2, 0:FREQ], ps[:, 0:FREQ]), ("AB", i))
            for dd in range(2):
                ps = filled(dve, ("kendT", dd))
                free_bank(dve.tensor_copy(kend_tok[:, dd].rearrange("p t n -> p (t n)"), ps[:, :]), ("kendT", dd))
            for dd in range(2):
                ps = [filled(dve, ("kv", dd, odd)) for odd in range(2)]
                order = range(NCH - 1) if dd == 0 else range(NCH - 1, 0, -1)
                for i, n in enumerate(order):
                    to = n + 1 if dd == 0 else n - 1
                    kv = ps[n % 2][:, n // 2 * GDV:(n // 2 + 1) * GDV]
                    if i == 0:
                        ins = dve.tensor_copy(state[:, dd, to, :], kv)
                    else:
                        ins = dve.scalar_tensor_tensor(state[:, dd, to, :], state[:, dd, n, :], dec[:, dd, n:n + 1], kv,
                                                       ALU.mult, ALU.add)
                    if i < NCH - 3:
                        link(ins)
                    else:
                        free_bank(ins, ("kv", dd, n % 2))
                        drained(dve, ("kv", dd, n % 2))
            dve.wait_ge(att_zero, 1)
            for t in range(T):
                for dd in range(2):
                    ps = filled(dve, ("att", t, dd))
                    ins = dve.copy_predicated(att[:, t], mask[:, dd, :].unsqueeze(1).to_broadcast([P, GH, P]),
                                              ps[:, :].rearrange("p (h n) -> p h n", h=GH))
                    free_bank(ins, ("att", t, dd))
                    drained(dve, ("att", t, dd))
            for h in range(1, MH, 2):
                ps = filled(dve, ("qT", h))
                free_bank(dve.tensor_copy(qT[0:QD, h, :], ps[0:QD, :]), ("qT", h))
            for t in range(T):
                dve.wait_ge(squares_ready, T + 8 + t + 1)
                link(dve.tensor_reduce(rgla[:, 3, t * GH:(t + 1) * GH], osq[:, t].rearrange("p (h v) -> p h v", h=GH),
                                       AX, ALU.add))
            variance(rgla[:, 0], rgla[:, 3], GDV)
            dve.wait_ge(var_ready, norms[0])
            refine(rgla[:, 1], rgla[:, 0], rgla[:, 2])
            for t in range(T):
                ps = filled(dve, ("o", t))
                free_bank(dve.tensor_tensor(MIX[:, t, 0:256].rearrange("p (h v) -> p h v", h=GH),
                                            ps[:, 0:GH * GDV].rearrange("p (h v) -> p h v", h=GH),
                                            rgla[:, 1, t * GH:(t + 1) * GH].unsqueeze(2).to_broadcast([P, GH, GDV]),
                                            ALU.mult), ("o", t))
            def normalise(i):
                drained(dve, ("S", i))
                link(dve.reciprocal(ri[:, i:i + 1], rs[:, i:i + 1]))
                dve.tensor_scalar(probs[:, i % 4], probs[:, i % 4], ri[:, i:i + 1], None, ALU.mult).then_inc(norm_ready, 1)

            for i in range(T * MH + 6):
                if i < T * MH:
                    ps = filled(dve, ("S", i))
                    dve.tensor_reduce(nm[:, i:i + 1], ps[:, :], AX, ALU.max, negate=True).then_inc(neg_max, 1)
                if 1 <= i <= T * MH:
                    normalise(i - 1)
                if i == 2:
                    for c in range(1, 4, 2):
                        ps = filled(dve, ("mT", c))
                        free_bank(dve.tensor_copy(xnT[:, c, :], ps[:, :]), ("mT", c))
                tq = (i - 13) // MH
                if i >= 13 and (i - 13) % MH == 0:
                    ps = banks[PLAN[("O", tq)][0]]
                    dve.wait_ge(av_done, (tq + 1) * 4)
                    free_bank(dve.tensor_copy(xnT[:, 4:8, tq * P:(tq + 1) * P],
                                              ps[:, :].rearrange("p (c n) -> p c n", c=4)), ("O", tq))

            def first_max(vals, k, t, r, onehot, m):
                link(dve.tensor_reduce(m, vals, AX, ALU.max))
                a = rt[:, t, r, 0:k]
                b = rt[:, t, 0, 12:13]
                link(dve.scalar_tensor_tensor(a, vals, m, rank[:, 0:k], ALU.is_equal, ALU.mult))
                link(dve.tensor_reduce(b, a, AX, ALU.min))
                return dve.tensor_scalar(onehot, a, b, None, ALU.is_equal)

            def choose(first, buf):
                e = slice(first, first + 2) if isinstance(first, int) else bass.ds(first, 2)
                dve.tensor_tensor(sel[:, buf], pos1[:, :, e].unsqueeze(3).to_broadcast([P, T, 2, BLOCK]),
                                  small[:, ONE_UP:].unsqueeze(1).unsqueeze(1).to_broadcast([P, T, 2, BLOCK]),
                                  ALU.is_equal).then_inc(sel_ready, 1)

            for step in OUT_ORDER:
                kind, t = step[0:2]
                if kind == "out":
                    n = step[2]
                    ps = filled(dve, step)
                    xs = X[:, t, n * 512:(n + 1) * 512]
                    free_bank(dve.tensor_tensor(xs, ps[:, :], xs, ALU.add), step)
                    if n == 0:
                        continue
                    drained(dve, ("out", t, 0))
                    drained(dve, ("out", t, 1))
                    dve.wait_ge(squares_ready, SQ2 + 2 * t + 2)
                    dve.tensor_scalar(rn2[:, t, 1:2], rn2[:, t, 0:1], rn2[:, t, 4:5], EPS, ALU.add, ALU.add).then_inc(var_ready, 1)
                    norms[0] += 1
                    dve.wait_ge(var_ready, norms[0])
                    refine(rn2[:, t, 2:3], rn2[:, t, 1:2], rn2[:, t, 3:4])
                    if t == 0:
                        for c in range(4):
                            drained(dve, ("mT", c))
                        dve.wait_ge(g2_landed, 16)
                    dve.scalar_tensor_tensor(MIX[:, t, :].rearrange("p (c q) -> p q c", c=C),
                                             X[:, t, :].rearrange("p (q c) -> p q c", c=C), rn2[:, t, 2:3],
                                             g2b[:, :].rearrange("p (q c) -> p q c", c=C),
                                             ALU.mult, ALU.mult).then_inc(x2_ready, 1)
                elif kind == "T":
                    if t == T - 1:
                        ps = filled(dve, ("x2T", t, 1))
                        free_bank(dve.tensor_copy(xnT[:, 4:8, t * P:(t + 1) * P],
                                                  ps[:, :].rearrange("p (c n) -> p c n", c=4)), ("x2T", t, 1))
                elif kind == "L":
                    ps = filled(dve, step)
                    free_bank(dve.tensor_tensor(lg[:, t, :], ps[:, 0:NG + NE], rbias[:, :], ALU.add), step)
                    drained(dve, step)
                    sc = rt[:, t, 0]
                    ohg, l32 = rt[:, t, 2, 0:NG], rt[:, t, 4]
                    dve.tensor_reduce(sc[:, 3:4], lg[:, t, 0:NG], AX, ALU.max, negate=True).then_inc(logit_ready, 1)
                    link(first_max(lg[:, t, 0:NG], NG, t, 3, ohg, sc[:, 2:3]))
                    link(dve.tensor_scalar(ohg, ohg, -NBIG, NBIG, ALU.mult, ALU.add))
                    link(dve.tensor_tensor(l32.rearrange("p (g e) -> p g e", g=NG),
                                           lg[:, t, NG:].rearrange("p (g e) -> p g e", g=NG),
                                           ohg.unsqueeze(2).to_broadcast([P, NG, EPG]), ALU.add))
                    link(first_max(l32, NE, t, 8, oh[:, t, 0], sc[:, 6:7]))
                    link(dve.scalar_tensor_tensor(l32, oh[:, t, 0], 4 * NBIG, l32, ALU.mult, ALU.add))
                    link(first_max(l32, NE, t, 9, oh[:, t, 1], sc[:, 7:8]))
                    dve.tensor_tensor(mska[:, t], oh[:, t, 0], oh[:, t, 1], ALU.add).then_inc(picks_ready, 1)
                    dve.tensor_tensor(sc[:, 5:6], sc[:, 7:8], sc[:, 6:7], ALU.subtract).then_inc(logit_ready, 1)
                elif kind == "pos":
                    ps = filled(dve, step)
                    link(dve.scalar_tensor_tensor(pos1[:, t], ps[:, 0:NE], 1.0, mska[:, t], ALU.add, ALU.mult))
                    dve.tensor_tensor(sel0[:, t], pos1[:, t, 0:2].unsqueeze(2).to_broadcast([P, 2, BLOCK]),
                                      small[:, ONE_UP:].unsqueeze(1).to_broadcast([P, 2, BLOCK]),
                                      ALU.is_equal).then_inc(sel_ready, 1)
                    row, rows2 = rt[:, t, 10], rt[:, t, 11:13]
                    free_bank(dve.tensor_tensor(row, ps[:, 0:NE], small[:, 0:NE], ALU.add), step)
                    drained(dve, step)
                    link(dve.tensor_tensor(rows2, oh[:, t], row.unsqueeze(1).to_broadcast([P, 2, NE]), ALU.mult))
                    link(dve.tensor_reduce(rt[:, t, 0, 10:12], rows2, AX, ALU.add))
                    dve.tensor_copy(dest[:, t, :], rt[:, t, 0, 10:12]).then_inc(dest_ready, 1)
                    sc = rt[:, t, 0]
                    dve.wait_ge(rexp_ready, 2 * t + 2)
                    link(dve.tensor_scalar(sc[:, 8:9], sc[:, 4:5], 1.0, sc[:, 0:1], ALU.add, ALU.mult))
                    link(dve.reciprocal(wts[:, t, 0:1], sc[:, 8:9]))
                    link(dve.tensor_tensor(wts[:, t, 1:2], wts[:, t, 0:1], sc[:, 4:5], ALU.mult))
            ps = filled(dve, "count")
            free_bank(dve.tensor_reduce(lv[:, 0, 0:1], ps[:, 0:NE], AX, ALU.max), "count")
            drained(dve, "count")
            dve.tensor_copy(nmax[:, :], lv[:, 0, 0:1]).then_inc(nmax_ready, 1)

            choose(2, 1)
            ps = filled(dve, "listT")
            dve.wait_ge(nmax_ready, 1)
            free_bank(dve.tensor_copy(lv[:, 2], ps[:, 0:NE]), "listT")
            drained(dve, "listT")
            link(dve.tensor_scalar(lv[:, 0], lv[:, 2], float(S), -2.0 * S, ALU.is_ge, ALU.mult))
            link(dve.tensor_scalar(lv[:, 1], lv[:, 2], 2.0, small[:, 40:41], ALU.mult, ALU.add))
            link(dve.tensor_copy(sidx[:, :], lv[:, 1]))
            dve.tensor_tensor(gidx[:, :], lv[:, 1], lv[:, 0], ALU.add).then_inc(idx_ready, 1)

            def gated(e, slot):
                dve.wait_ge(silu_done, e + 1)
                if not (isinstance(e, int) and e < 2):
                    dve.wait_ge(hT_full, e - 1)
                dve.tensor_tensor(hg[:, slot % 2], hs[:, slot % 2], banks[2 + slot % 2][:, P:2 * P],
                                  ALU.mult).then_inc(hg_ready, 1)

            def copy_h(e, slot):
                dve.wait_ge(hT_full, e + 1)
                if not (isinstance(e, int) and e < 2):
                    dve.wait_ge(y_full, e - 1)
                dve.tensor_copy(hT[:, slot % 2].rearrange("p m s -> p (m s)"),
                                banks[6 + slot % 2][:, 0:P]).then_inc(hT_ready, 1)

            def copy_y(e, turn2, slot):
                dve.wait_ge(y_full, e + 1)
                if not (isinstance(e, int) and e < 2):
                    dve.wait_ge(y_stored[slot % 2], turn2 * 16)
                dve.tensor_copy(Y[:, slot % 2], banks[4 + slot % 2][:, :]).then_inc(y_ready, 1)

            def step(e, turn, s):
                known = isinstance(e, int)
                gated(e, s)
                if not (known and e < 1):
                    copy_y(e - 1, turn * (RING // 2) + (s - 1) // 2, (s - 1) % RING)
                copy_h(e, s)
                if s % 2 == 0 and not (known and (e + 4 >= NE or not picked(e // 2 + 2))):
                    dve.wait_ge(xe_full, e + 2)
                    choose(e + 4, s // 2)

            for e in range(2 * RING):
                step(e, e // RING, e % RING)
            with dve.Fori(2, NE // RING - 1) as i:
                for s in range(RING):
                    step(i * RING + s, i, s)
            for e in range(NE - RING, NE):
                step(e, NE // RING - 1, e % RING)
            copy_y(NE - 1, (NE - 1) // 2, RING - 1)
            dve.wait_ge(nmax_ready, 1)
            with dve.If(dve.value_load(nmax[0:1, 0:1]) > BLOCK):
                with dve.Fori(0, NE * OVB) as n:
                    dve.wait_ge(ov_list, n * 32 + 32)
                    dve.tensor_scalar(ovl[:, 1:2], ovl[:, 0:1], float(S), -2.0 * S, ALU.is_ge, ALU.mult).then_inc(ov_tmp, 1)
                    dve.tensor_scalar(ovl[:, 2:3], ovl[:, 0:1], 2.0, small[:, 40:41], ALU.mult, ALU.add).then_inc(ov_tmp, 1)
                    dve.wait_ge(ov_tmp, n * 2 + 2)
                    dve.tensor_copy(ov_s[:, :], ovl[:, 2:3]).then_inc(ov_idx, 1)
                    dve.tensor_tensor(ov_g[:, :], ovl[:, 2:3], ovl[:, 1:2], ALU.add).then_inc(ov_idx, 1)
                    dve.wait_ge(ov_silu, n + 1)
                    dve.tensor_tensor(hg[:, 0], hs[:, 0], banks[2][:, P:2 * P], ALU.mult).then_inc(ov_hg, 1)
                    dve.wait_ge(ov_hT, n + 1)
                    dve.tensor_copy(hT[:, 0].rearrange("p m s -> p (m s)"), banks[6][:, 0:P]).then_inc(ov_hc, 1)
                    dve.wait_ge(ov_y, n + 2)
                    dve.tensor_copy(Y[:, 0], banks[4][:, :]).then_inc(ov_yc, 1)

            def mean_square(t):
                dve.wait_ge(squares_ready, SQ3 + t + 1)
                variance(stat[:, 52 + t:53 + t], stat[:, 48 + t:49 + t], D)
                dve.wait_ge(var_ready, norms[0])

            def root(t):
                dve.wait_ge(guess_ready, norms[0])
                guess, tmp = stat[:, 56 + t:57 + t], stat[:, 60 + t:61 + t]
                link(dve.tensor_tensor(tmp, guess, guess, ALU.mult))
                link(dve.scalar_tensor_tensor(tmp, tmp, -0.5, stat[:, 52 + t:53 + t], ALU.mult, ALU.mult))
                dve.scalar_tensor_tensor(guess, tmp, 1.5, guess, ALU.add, ALU.mult).then_inc(root_ready, 1)

            for t in range(T):
                dve.wait_ge(pair_landed[t][0], 16)
                link(dve.scalar_tensor_tensor(X[:, t, :], ypair[:, t, 0], wts[:, t, 0:1], X[:, t, :], ALU.mult, ALU.add))
                if t >= 1:
                    mean_square(t - 1)
                dve.wait_ge(pair_landed[t][1], 16)
                dve.scalar_tensor_tensor(X[:, t, :], ypair[:, t, 1], wts[:, t, 1:2], X[:, t, :],
                                         ALU.mult, ALU.add).then_inc(x3_ready, 1)
                if t >= 1:
                    root(t - 1)
            mean_square(T - 1)
            root(T - 1)

        @block.gpsimd
        def _(pool):
            link = linker(pool, pool_chain)

            def hold():
                pool.tensor_tensor(held[:, 0:1], held[:, 1:2], held[:, 1:2], ALU.add).then_inc(held_done, 1)

            pool.memset(held[:, :], 0.0).then_inc(held_done, 1)
            pool.memset(wa[:, :, :], 0.0).then_inc(gatew_zero, 1)
            pool.memset(wr[:, :, :], 0.0).then_inc(gatew_zero, 1)
            link(pool.memset(keep, 1.0))
            pool.memset(keep.rearrange("p (n s) -> p n s", s=CHUNK)[:, :, 0:1], 0.0).then_inc(keep_ready, 1)
            link(pool.memset(krp[:, :, 0:NOPE], 0.0))
            pool.memset(lfill[:, :], EMPTY).then_inc(fill_ready, 1)
            for t in range(T):
                drained(pool, ("vg", t))
            pool.memset(fw, 0.0).then_inc(fnetw_zero, 1)
            pool.memset(att.rearrange("p t h n -> p (t h n)"), 0.0).then_inc(att_zero, 1)

            def rotate(x1, x2, o1, o2, sin, cos, t1, t2, t3, t4):
                link(pool.tensor_tensor(t1, x1, cos, ALU.mult))
                link(pool.tensor_tensor(t2, x2, sin, ALU.mult))
                link(pool.tensor_tensor(t3, x1, sin, ALU.mult))
                link(pool.tensor_tensor(t4, x2, cos, ALU.mult))
                link(pool.tensor_tensor(o1, t1, t2, ALU.subtract))
                return pool.tensor_tensor(o2, t3, t4, ALU.add)

            pool.wait_ge(tables_ready, 2)
            for t in range(T):
                drained(pool, ("ckr", t))
            k1, k2 = ckr[:, :, 128:144], ckr[:, :, 144:160]
            tm = [rtmp[:, i].rearrange("p h w -> p (h w)")[:, 0:T * HALF].rearrange("p (t w) -> p t w", t=T) for i in range(4)]
            rotate(k1, k2, krp[:, :, NOPE:NOPE + HALF], krp[:, :, NOPE + HALF:], ropet[:, 0], ropet[:, 1],
                   *tm).then_inc(kr_rot, 1)
            pool.wait_ge(kr_rot, 1)
            for t in range(T):
                drained(pool, ("q", t, 0))
                drained(pool, ("q", t, 1))
                q1, q2 = qs[:, t, :, NOPE:NOPE + HALF], qs[:, t, :, NOPE + HALF:]
                sin = ropet[:, 0, t, :].unsqueeze(1).to_broadcast([P, MH, HALF])
                cos = ropet[:, 1, t, :].unsqueeze(1).to_broadcast([P, MH, HALF])
                rotate(q1, q2, q1, q2, sin, cos, *[rtmp[:, i] for i in range(4)]).then_inc(q_rot, 1)
                pool.wait_ge(q_rot, t + 1)
            for i in range(4):
                drained(pool, ("AB", i))
            pool.memset(WO[:, 0:4096], 0.0).then_inc(diag_zero, 1)
            for t in range(T):
                drained(pool, ("fy", t))
            for dd in range(2):
                drained(pool, ("kendT", dd))
            pool.memset(WO[:, 4096:], 0.0).then_inc(diag_zero, 1)
            for t in range(T):
                drained(pool, ("o", t))
            pool.tensor_tensor(MIX[:, :, 0:256], MIX[:, :, 0:256], vg[:, :, 256:512], ALU.mult).then_inc(gla_out, 1)
            pool.wait_ge(list_filled, 16)
            for t in range(T):
                pool.wait_ge(dest_ready, t + 1)
                for r in range(2):
                    pool.indirect_dma_start(list_d, bass.IndirectOffsetOnAxis(ap=dest[:, t, r:r + 1], axis=0),
                                            small[:, 41 + 2 * t + r:42 + 2 * t + r], None,
                                            bounds_check=NE * S - 1, oob_is_err=False).then_inc(scattered, 16)
            pool.wait_ge(idx_ready, 1)

            def scatter(e):
                pool.wait_ge(y_ready, e + 1)
                pool.indirect_dma_start(y_rows, bass.IndirectOffsetOnAxis(ap=sidx[:, e:e + 1], axis=0),
                                        Y[:, e % 2], None,
                                        bounds_check=4 * S - 1, oob_is_err=False).then_inc(y_stored[e % 2], 16)

            def gather(e):
                if e >= 2 * GATHERED[0] + 2:
                    pool.wait_ge(xe_full, e - 1)
                pool.indirect_dma_start(xg[e % 2], None, x2_rows,
                                        bass.IndirectOffsetOnAxis(ap=gidx[:, e:e + 1], axis=0),
                                        bounds_check=2 * S - 1, oob_is_err=False).then_inc(xg_landed[e % 2], 16)

            pool.wait_ge(x2_stored, 16 * T)
            gathers = list(range(2 * GATHERED[0], 2 * GATHERED[-1] + 2))
            for e in gathers[:2]:
                gather(e)
            for e in range(NE):
                scatter(e)
                if e + 2 < len(gathers):
                    gather(gathers[e + 2])
            for q in range(2):
                pool.wait_ge(y_stored[q], 16 * NE // 2)
            pool.wait_ge(nmax_ready, 1)
            with pool.If(pool.value_load(nmax[0:1, 0:1]) > BLOCK):
                with pool.Fori(0, NE * OVB) as n:
                    pool.wait_ge(held_done, n * 3 + 1)
                    pool.wait_ge(ov_idx, n * 2 + 2)
                    hold()
                    pool.indirect_dma_start(xg[0], None, x2_rows,
                                            bass.IndirectOffsetOnAxis(ap=ov_g[:, 0:1], axis=0),
                                            bounds_check=2 * S - 1, oob_is_err=False).then_inc(ov_x, 16)
                    pool.wait_ge(held_done, n * 3 + 2)
                    pool.wait_ge(ov_yc, n + 1)
                    hold()
                    pool.indirect_dma_start(y_rows, bass.IndirectOffsetOnAxis(ap=ov_s[:, 0:1], axis=0),
                                            Y[:, 0], None,
                                            bounds_check=4 * S - 1, oob_is_err=False).then_inc(ov_stored, 16)
                    pool.wait_ge(held_done, n * 3 + 3)
                    pool.wait_ge(ov_stored, n * 16 + 16)
                    hold()
                pool.wait_ge(held_done, NE * OVB * 3 + 1)
            pool.nop().then_inc(moe_done, 1)
            pool.wait_ge(gf_landed, 16)
            for t in range(T):
                pool.wait_ge(x3_ready, t + 1)
                pool.tensor_tensor(MIX[:, t, :], X[:, t, :], gfb, ALU.mult).then_inc(x3_gain, 1)


_INS = ["x", "positions", "norm1_g", "w_in", "gla_wa_f", "gla_ba_f", "gla_wa_b", "gla_ba_b", "gla_norm_g", "fnet_w",
        "mla_q_norm_g", "mla_w_uq", "mla_kv_norm_g", "mla_w_ukv", "w_out", "norm2_g", "moe_w_rg", "moe_b_rg",
        "moe_w_re", "moe_b_re", "moe_w_gate", "moe_w_up", "moe_w_down", "final_norm_g"]


def kernel(**inputs):
    import numpy as _np
    import concourse.bacc as _bacc
    from concourse import mybir as _mybir
    from concourse.bass_utils import run_bass_kernel_spmd as _run

    nc = _bacc.Bacc("TRN2", target_bir_lowering=False, num_devices=1)
    given = {name: _np.ascontiguousarray(inputs[name]) for name in _INS}
    given.update(shape_constants())
    arrays, aps = {}, {}
    for name, a in given.items():
        arrays[f"in_{name}"] = a
        aps[name] = nc.dram_tensor(f"in_{name}", a.shape, _mybir.dt.from_np(a.dtype), kind="ExternalInput").ap()
    out = nc.dram_tensor("out_0", (1, S, D), F32, kind="ExternalOutput").ap()
    encoder_kernel(nc, aps, out)
    return _run(nc, [arrays], core_ids=[0]).results[0]["out_0"]
```
